# Optimizing a Trainium2 kernel written in Bass

```python
import math
import jax, jax.numpy as jnp
from jax import lax
import numpy as np

D_MODEL = 1024
BATCH = 1
SEQ = 512
DEPTH = 2
DEC_BATCH = 8
DEC_SEQ = 8
PAST_LEN = 4096
PAGE_SIZE = 128

N_MEM = 256
D_CONV = D_MODEL
CONV_W = 3
D_SG = D_MODEL
SG_GROUPS = 8
SG_GROUP_DIM = D_SG // SG_GROUPS
CHUNK = 128
X_HEADS = 4
X_HEAD_DIM = D_MODEL // X_HEADS
N_KEYS = 128
N_EXPERTS = N_KEYS * N_KEYS
PEER_HEADS = 8
PEER_TOPK = 16
PEER_QDIM = 256
PEER_HALF = PEER_QDIM // 2
PEER_BLOCK = 128
EPS = 1e-6
N_IN = 3 * D_CONV + 2 * D_SG + 2 * D_MODEL
SPLITS = (D_CONV, 2 * D_CONV, 3 * D_CONV, 3 * D_CONV + D_SG, 3 * D_CONV + 2 * D_SG,
          3 * D_CONV + 2 * D_SG + D_MODEL)

kernel_name = 'hybrid_conv_sgu_peer_decoder_step'

def _rmsnorm(x, g):
    xf = x.astype(jnp.float32)
    y = xf * lax.rsqrt(jnp.mean(xf * xf, axis=-1, keepdims=True) + EPS)
    return (y * g).astype(x.dtype)

def _layernorm(x, g, b):
    xf = x.astype(jnp.float32)
    mu = jnp.mean(xf, axis=-1, keepdims=True)
    var = jnp.mean(jnp.square(xf - mu), axis=-1, keepdims=True)
    return ((xf - mu) * lax.rsqrt(var + EPS) * g + b).astype(x.dtype)

def _spatial_gate(vn, sg_w, sg_b):
    bn, L, _ = vn.shape
    c = min(CHUNK, L)
    n = L // c
    vr = vn.reshape(bn, n, c, SG_GROUPS, SG_GROUP_DIM)
    mask = jnp.tril(jnp.ones((c, c), dtype=bool))
    w = jnp.where(mask, sg_w[:, :c, :c], 0).astype(vn.dtype)
    mixed = jnp.einsum('gts,bnsgd->bntgd', w, vr) + sg_b[:, :c].T[:, :, None].astype(vn.dtype)
    return mixed.reshape(bn, L, D_SG)

def _mixer(h, conv_buf, p):
    proj = jnp.einsum('bld,dn->bln', h, p['w_in'])
    b_g, c_g, h_a, u, v, g_a, g_b = jnp.split(proj, SPLITS, axis=-1)
    z = c_g * h_a
    L = z.shape[1]
    zp = jnp.concatenate([conv_buf.astype(z.dtype), z], axis=1)
    conv = sum(p['conv_w'][j] * zp[:, j:j + L] for j in range(CONV_W))
    new_buf = zp[:, L:]
    o_a = jnp.einsum('blc,cd->bld', b_g * conv, p['w_a_out'])
    u = jax.nn.gelu(u)
    vn = _layernorm(jax.nn.gelu(v), p['sg_ln_g'], p['sg_ln_b'])
    s = _spatial_gate(vn, p['sg_w'], p['sg_b'])
    o_b = jnp.einsum('blc,cd->bld', u * s, p['w_b_out'])
    m = jax.nn.sigmoid(g_a) * o_a + jax.nn.sigmoid(g_b) * o_b
    return jnp.einsum('bld,de->ble', m, p['w_mix_o']), new_buf, vn

def _mem_kv(mem, g_mem, w_k, w_v):
    m = _rmsnorm(mem, g_mem)
    bn = mem.shape[0]
    k = jnp.einsum('bmd,de->bme', m, w_k).reshape(bn, N_MEM, X_HEADS, X_HEAD_DIM)
    v = jnp.einsum('bmd,de->bme', m, w_v).reshape(bn, N_MEM, X_HEADS, X_HEAD_DIM)
    return k, v

def _cross_attn(h, mem_k, mem_v, w_q, w_o):
    bn, L, _ = h.shape
    q = jnp.einsum('bld,de->ble', h, w_q).reshape(bn, L, X_HEADS, X_HEAD_DIM)
    s = jnp.einsum('blhe,bmhe->bhlm', q, mem_k.astype(q.dtype)).astype(jnp.float32) / math.sqrt(X_HEAD_DIM)
    pr = jax.nn.softmax(s, axis=-1).astype(h.dtype)
    o = jnp.einsum('bhlm,bmhe->blhe', pr, mem_v.astype(h.dtype)).reshape(bn, L, D_MODEL)
    return jnp.einsum('bld,de->ble', o, w_o)

def _peer(h, w_pq, sub_keys, peer_u, peer_v):
    bn, L, D = h.shape
    t = h.reshape(-1, D)
    T = t.shape[0]
    q = jnp.einsum('td,de->te', t, w_pq).reshape(T, PEER_HEADS, 2, PEER_HALF)
    s = jnp.einsum('thpk,hpnk->thpn', q, sub_keys.astype(q.dtype)).astype(jnp.float32)
    s1, i1 = lax.top_k(s[:, :, 0], PEER_TOPK)
    s2, i2 = lax.top_k(s[:, :, 1], PEER_TOPK)
    cand = (s1[..., :, None] + s2[..., None, :]).reshape(T, PEER_HEADS, PEER_TOPK * PEER_TOPK)
    cidx = (i1[..., :, None] * N_KEYS + i2[..., None, :]).reshape(T, PEER_HEADS, PEER_TOPK * PEER_TOPK)
    top_s, pos = lax.top_k(cand, PEER_TOPK)
    idx = jnp.take_along_axis(cidx, pos, axis=-1).reshape(T, PEER_HEADS * PEER_TOPK)
    g = jax.nn.softmax(top_s, axis=-1).reshape(T, PEER_HEADS * PEER_TOPK).astype(t.dtype)
    pad = (-T) % PEER_BLOCK
    tp = jnp.pad(t, ((0, pad), (0, 0))).reshape(-1, PEER_BLOCK, D)
    ip = jnp.pad(idx, ((0, pad), (0, 0))).reshape(-1, PEER_BLOCK, PEER_HEADS * PEER_TOPK)
    gp = jnp.pad(g, ((0, pad), (0, 0))).reshape(-1, PEER_BLOCK, PEER_HEADS * PEER_TOPK)

    def block(args):
        tb, ib, gb = args
        ue = jnp.take(peer_u, ib, axis=0).astype(tb.dtype)
        a = jax.nn.gelu(jnp.einsum('td,ted->te', tb, ue))
        ve = jnp.take(peer_v, ib, axis=0).astype(tb.dtype)
        return jnp.einsum('te,ted->td', gb * a, ve)

    out = lax.map(block, (tp, ip, gp)).reshape(-1, D)[:T]
    return out.reshape(bn, L, D)

def _layer(x, conv_buf, mem_k, mem_v, p):
    mo, new_buf, vn = _mixer(_rmsnorm(x, p['g_mix']), conv_buf, p)
    x = x + mo
    x = x + _cross_attn(_rmsnorm(x, p['g_xattn']), mem_k, mem_v, p['w_xq'], p['w_xo'])
    x = x + _peer(_rmsnorm(x, p['g_ffn']), p['w_pq'], p['sub_keys'], p['peer_u'], p['peer_v'])
    return x, new_buf, vn

def setup_inputs(seed: int = 0) -> dict:
    key = jax.random.key(seed)
    ks = jax.random.split(key, 32)
    f32 = jnp.float32

    def nrm(k, shape, scale):
        return jax.random.normal(k, shape, f32) * scale

    def gain(k, shape):
        return 1.0 + 0.01 * jax.random.normal(k, shape, f32)

    return {
        'x_prompt': nrm(ks[0], (BATCH, SEQ, D_MODEL), 1.0),
        'x_sample': nrm(ks[1], (DEC_BATCH, DEC_SEQ, D_MODEL), 1.0),
        'state_conv': nrm(ks[2], (DEPTH, DEC_BATCH, CONV_W - 1, D_CONV), 0.5),
        'cache_mem_k': nrm(ks[3], (DEPTH, DEC_BATCH, N_MEM, X_HEADS, X_HEAD_DIM), 1.0),
        'cache_mem_v': nrm(ks[4], (DEPTH, DEC_BATCH, N_MEM, X_HEADS, X_HEAD_DIM), 1.0),
        'mem_prompt': nrm(ks[5], (BATCH, N_MEM, D_MODEL), 1.0),
        'g_mix': gain(ks[6], (DEPTH, D_MODEL)),
        'w_in': nrm(ks[7], (DEPTH, D_MODEL, N_IN), D_MODEL ** -0.5),
        'conv_w': nrm(ks[8], (DEPTH, CONV_W, D_CONV), CONV_W ** -0.5),
        'w_a_out': nrm(ks[9], (DEPTH, D_CONV, D_MODEL), D_CONV ** -0.5),
        'sg_ln_g': gain(ks[10], (DEPTH, D_SG)),
        'sg_ln_b': nrm(ks[11], (DEPTH, D_SG), 0.01),
        'sg_w': nrm(ks[12], (DEPTH, SG_GROUPS, CHUNK, CHUNK), CHUNK ** -0.5),
        'sg_b': 1.0 + nrm(ks[13], (DEPTH, SG_GROUPS, CHUNK), 0.01),
        'w_b_out': nrm(ks[14], (DEPTH, D_SG, D_MODEL), D_SG ** -0.5),
        'w_mix_o': nrm(ks[15], (DEPTH, D_MODEL, D_MODEL), D_MODEL ** -0.5),
        'g_xattn': gain(ks[16], (DEPTH, D_MODEL)),
        'g_mem': gain(ks[17], (DEPTH, D_MODEL)),
        'w_xq': nrm(ks[18], (DEPTH, D_MODEL, D_MODEL), D_MODEL ** -0.5),
        'w_xk': nrm(ks[19], (DEPTH, D_MODEL, D_MODEL), D_MODEL ** -0.5),
        'w_xv': nrm(ks[20], (DEPTH, D_MODEL, D_MODEL), D_MODEL ** -0.5),
        'w_xo': nrm(ks[21], (DEPTH, D_MODEL, D_MODEL), D_MODEL ** -0.5),
        'g_ffn': gain(ks[22], (DEPTH, D_MODEL)),
        'w_pq': nrm(ks[23], (DEPTH, D_MODEL, PEER_HEADS * PEER_QDIM), D_MODEL ** -0.5),
        'sub_keys': nrm(ks[24], (DEPTH, PEER_HEADS, 2, N_KEYS, PEER_HALF), PEER_HALF ** -0.5),
        'peer_u': nrm(ks[25], (DEPTH, N_EXPERTS, D_MODEL), D_MODEL ** -0.5),
        'peer_v': nrm(ks[26], (DEPTH, N_EXPERTS, D_MODEL), PEER_HEADS ** -0.5),
        'g_final': gain(ks[27], (D_MODEL,)),
    }

def reference(x_prompt, x_sample, state_conv, cache_mem_k, cache_mem_v, mem_prompt,
              g_mix, w_in, conv_w, w_a_out, sg_ln_g, sg_ln_b, sg_w, sg_b, w_b_out, w_mix_o,
              g_xattn, g_mem, w_xq, w_xk, w_xv, w_xo,
              g_ffn, w_pq, sub_keys, peer_u, peer_v, g_final):
    xp, xs = x_prompt, x_sample
    conv_p, mk_p, mv_p, conv_s, sgv_s = [], [], [], [], []
    for l in range(DEPTH):
        p = dict(g_mix=g_mix[l], w_in=w_in[l], conv_w=conv_w[l], w_a_out=w_a_out[l],
                 sg_ln_g=sg_ln_g[l], sg_ln_b=sg_ln_b[l], sg_w=sg_w[l], sg_b=sg_b[l],
                 w_b_out=w_b_out[l], w_mix_o=w_mix_o[l], g_xattn=g_xattn[l],
                 w_xq=w_xq[l], w_xo=w_xo[l], g_ffn=g_ffn[l], w_pq=w_pq[l],
                 sub_keys=sub_keys[l], peer_u=peer_u[l], peer_v=peer_v[l])
        mk, mv = _mem_kv(mem_prompt, g_mem[l], w_xk[l], w_xv[l])
        zero_buf = jnp.zeros((xp.shape[0], CONV_W - 1, D_CONV), xp.dtype)
        xp, nb_p, _ = _layer(xp, zero_buf, mk, mv, p)
        conv_p.append(nb_p)
        mk_p.append(mk)
        mv_p.append(mv)
        xs, nb_s, vn_s = _layer(xs, state_conv[l], cache_mem_k[l], cache_mem_v[l], p)
        conv_s.append(nb_s)
        sgv_s.append(vn_s)
    y_prompt = _rmsnorm(xp, g_final)
    y_sample = _rmsnorm(xs, g_final)
    new_state_conv_p = jnp.stack(conv_p)
    new_mem_k_p = jnp.stack(mk_p)
    new_mem_v_p = jnp.stack(mv_p)
    new_state_conv_s = jnp.stack(conv_s)
    new_sg_v_s = jnp.stack(sgv_s)
    return (y_prompt, y_sample, new_state_conv_p, new_mem_k_p, new_mem_v_p, new_state_conv_s, new_sg_v_s)


_drawn_inputs = setup_inputs


def setup_inputs(seed=0):
    import zlib

    import numpy as np

    out = dict(_drawn_inputs(seed))
    spreads = {}
    factors = {'sg_ln_g': 3.119,
     'sg_ln_b': 4.023,
     'sg_b': 2.93,
     'g_xattn': 3.632,
     'g_mem': 4.733,
     'g_final': 38.063,
     'g_ffn': 3.34}
    for name, (base, spread) in spreads.items():
        noise = np.random.default_rng([zlib.crc32(name.encode()), seed]).standard_normal(out[name].shape)
        drawn = base * np.exp(spread * noise) if base else spread * noise
        out[name] = __import__('jax').numpy.asarray(drawn.astype(out[name].dtype))
    for name, factor in factors.items():
        out[name] = (out[name] * factor).astype(out[name].dtype)
    return out
```

```python
from contextlib import ExitStack

import concourse.bass as bass
from concourse import mybir

P = 128
DM = 1024
KC = DM // P
SEQ, NSEQ, NDEC = 512, 8, 8
NS = NSEQ * NDEC
NT = SEQ + NS
TILES = [(t, P) for t in range(SEQ // P)] + [(SEQ // P, NS)]
NTILE = len(TILES)
HALF = NT // 2
DEPTH, CW = 2, 3
HEADS, HD, NMEM = 4, 256, 256
MC = NMEM // P
PH, NK, TOPK = 8, 128, 16
NE = NK * NK
NSEL = PH * TOPK
EPS = 1e-6
UW = 256
SLOTS = 8
UF = KC * UW
GRP = 8
NGRP = NSEL // GRP
LOWEST = -3.0e38

F32 = mybir.dt.float32
U32 = mybir.dt.uint32
I32 = mybir.dt.int32
ALU = mybir.AluOpType
ACT = mybir.ActivationFunctionType
AX = mybir.AxisListType.X


def plan_jobs():
    jobs = [("par", "act"), ("st", "act"), ("sw", "dve"), ("sw64", "dve")]
    jobs += [(("n", 0, t), "dve") for t in range(NTILE)]
    jobs += [(("v", t), "act") for t in range(NTILE)]
    for c in range(KC):
        jobs += [(("c", c), "act"), (("h", c), "dve"), (("b", c), "dve"), (("u", c), "act")]
    jobs += [("zo", "act")]
    jobs += [(("mx", g), "dve") for g in range(KC)]
    for c in range(KC):
        jobs += [(("ga", c), "act"), (("oa", c), "dve"), (("gb", c), "act"), (("ob", c), "dve")]
    jobs += [(("mo", t), "dve") for t in range(NTILE)]
    jobs += [(("mt", m), "dve") for m in range(MC)]
    jobs += [(("k", m), "act") for m in range(MC)]
    jobs += [(("vv", m), "act") for m in range(MC)]
    jobs += [(("kt", m), "dve") for m in range(MC)]
    jobs += [(("n", 1, t), "dve") for t in range(NTILE)]
    jobs += [(("q", c), "act") for c in range(KC)]
    for t in range(SEQ // P):
        jobs += [(("s", t), "act")]
        if t:
            jobs += [(("pt", t - 1), "act")]
    jobs += [(("kb", 0, m), ("act", "dve")[m]) for m in range(MC)]
    jobs += [(("pt", SEQ // P - 1), "act")]
    for b in range(1, NSEQ):
        jobs += [(("kb", b, m), ("act", "dve")[m]) for m in range(MC)]
    jobs += [("ss", "act")]
    jobs += [(("o", c), "act") for c in range(KC)]
    jobs += [(("pt", 4), "act"), ("os", "dve")]
    jobs += [(("xo", t), "dve") for t in range(NTILE)]
    jobs += [("sk0", "dve"), ("sk1", "dve")]
    jobs += [(("n", 2, t), "dve") for t in range(NTILE)]
    jobs += [(("pq", 0), "act"), (("pq", 1), "act")]
    for h in range(PH):
        if h + 1 < PH:
            jobs += [(("pq", 2 * h + 2), "act"), (("pq", 2 * h + 3), "act")]
        jobs += [(("sc", h, 0), "act"), (("sc", h, 1), "act")]
    index, pair, before, turn = {}, {}, {}, {}
    last, counts, cursor = {}, {"act": 0, "dve": 0}, 0
    for i, (name, owner) in enumerate(jobs):
        index[name] = i
        if name == "ss":
            p = 3
        else:
            held = ("kb", 0, 0) in index and "ss" not in index
            while held and cursor % 4 == 3:
                cursor += 1
            p = cursor % 4
            cursor += 1
        pair[name], before[name], last[p] = p, last.get(p), name
        counts[owner] += 1
        turn[name] = counts[owner]
    return jobs, index, pair, before, turn


def plan_units(index):
    units, last = [], []

    def add(kind, n, job):
        units.append((kind, n))
        last.append(index[job])

    for n in range(4):
        add("v", n, ("v", NTILE - 1))
    for n in range(4):
        for kind in "chbu":
            add(kind, n, (kind, 2 * n + 1))
    for n in range(4):
        for kind in ("ga", "oa", "gb", "ob"):
            add(kind, n, (kind, 2 * n + 1))
    for n in range(4):
        add("mo", n, ("mo", NTILE - 1))
    for n in range(4):
        add("k", n, ("k", MC - 1))
    for n in range(4):
        add("vv", n, ("vv", MC - 1))
    for n in range(4):
        add("q", n, ("q", 2 * n + 1))
    for b in range(NSEQ):
        add("kb", b, ("kb", b, MC - 1))
    for b in range(NSEQ):
        add("vb", b, "os")
    for n in range(4):
        add("xo", n, ("xo", NTILE - 1))
    for h in range(PH):
        add("pq", h, ("pq", 2 * h + 1))
    assert len(units) % SLOTS == 0
    return units, last


def decoder_step(nc, A, O):
    jobs, JOB, PAIR, BEFORE, TURN = plan_jobs()
    units, unit_last = plan_units(JOB)
    UNIT = {u: i for i, u in enumerate(units)}
    owner = dict(jobs)

    with ExitStack() as ctx:
        def sb(name, shape, dt=F32):
            return ctx.enter_context(nc.sbuf_tensor(name, shape, dt))

        def sem(name):
            s = ctx.enter_context(nc.semaphore(name))
            sems.append(s)
            return s

        sems = []
        X = sb("X", [P, NTILE, DM])
        RH = sb("RH", [P, KC * NT])
        RB = sb("RB", [P, 10 * DM])
        RV = sb("RV", [P, NTILE * DM])
        W = sb("W", [P, SLOTS * UF])
        KV = sb("KV", [P, 4 * DM])
        TMP = sb("TMP", [P, 2400])
        ident = sb("ident", [P, P])
        tri = sb("tri", [P, P])
        tri64 = sb("tri64", [NS, NS])
        iota16 = sb("iota16", [P, TOPK])
        iota_i = sb("iota_i", [P, TOPK], I32)
        eps = sb("eps", [P, 1])
        row0 = sb("row0", [P, 1])
        PAR = sb("PAR", [6 * KC, P])
        PARC = sb("PARC", [P, 6 * KC])
        stT = sb("stT", [P, KC, 2 * NSEQ])
        zl = sb("zl", [P, KC, 2 + 2 * NSEQ])
        ssq = sb("ssq", [P, 8])
        std = sb("std", [P, 8])
        rstd = sb("rstd", [P, 8])
        bns = sb("bns", [P, NTILE, 2, 6])
        bna = sb("bna", [P, NTILE, 2])
        rmax = sb("rmax", [P, NTILE, HEADS])
        nmax = sb("nmax", [P, NTILE, HEADS])
        rsum = sb("rsum", [P, NTILE, HEADS])
        rinv = sb("rinv", [P, NTILE, HEADS])
        m16 = sb("m16", [P, 2 * PH, TOPK])
        i16 = sb("i16", [P, 2 * PH, TOPK], U32)
        i16f = sb("i16f", [P, 2 * PH, TOPK])
        tops = sb("tops", [P, PH, TOPK])
        pos = sb("pos", [P, 2, NSEL], U32)
        posf = sb("posf", [P, 2, NSEL])
        sel = sb("sel", [P, 2, NSEL])
        gsum = sb("gsum", [P, PH])
        ginv = sb("ginv", [P, PH])
        gate = sb("gate", [P, NSEL])
        idx = sb("idx", [P, NSEL], U32)
        idxg = sb("idxg", [P, GRP], U32)
        dots = sb("dots", [P, GRP])
        gel = sb("gel", [P, GRP])
        wts = sb("wts", [P, GRP])
        ps = ctx.enter_context(nc.psum_tensor("ps", [P, 8, 512], F32))

        hT = RH[:, :].rearrange("p (c n) -> p c n", c=KC)
        qmask = hT
        F1 = RB[:, 0:KC * NT].rearrange("p (c n) -> p c n", c=KC)
        F2 = RB[:, KC * NT:2 * KC * NT].rearrange("p (c n) -> p c n", c=KC)
        ln_g = RB[:, 9 * DM:10 * DM]
        sgw = RB[:, 0:DM].rearrange("p (g s) -> p g s", g=KC)
        sgw8 = RB[0:NS, DM:DM + 64].rearrange("p (g s) -> p g s", g=KC)
        sgw64 = RB[0:NS, DM + 64:DM + 64 + 8 * NS].rearrange("p (g s) -> p g s", g=KC)
        state = RB[0:2 * NSEQ, KC * NT:KC * NT + DM]
        mem = RB[:, 0:2 * DM].rearrange("p (m d) -> p m d", m=MC)
        memT = RB[:, 2 * DM:4 * DM].rearrange("p (c n) -> p c n", c=KC)
        ktok = RB[:, KC * NT:KC * NT + 2 * DM].rearrange("p (m d) -> p m d", m=MC)
        qT, oT = F1, F2
        S = RB[:, :].rearrange("p (t n) -> p t n", t=NTILE)
        XN = RV[:, :].rearrange("p (t d) -> p t d", t=NTILE)
        VT = XN
        mT = RV[:, 0:KC * NT].rearrange("p (c n) -> p c n", c=KC)
        PT = RV[:, 0:8 * SEQ].rearrange("p (i n) -> p i n", i=8)
        probs = [RV[:, 8 * SEQ:8 * SEQ + DM], RB[:, 9 * DM:10 * DM]]
        sgT = KV[:, 0:DM].rearrange("p (g t) -> p g t", g=KC)
        sgT64 = KV[0:NS, DM:DM + 8 * NS].rearrange("p (g t) -> p g t", g=KC)
        sg_b = KV[:, 1536:2560].rearrange("p (g t) -> p g t", g=KC)
        ln_b = KV[:, 2560:3584]
        kT = KV[:, 0:2 * DM].rearrange("p (c n) -> p c n", c=KC)
        vmem = KV[:, 2 * DM:4 * DM].rearrange("p (m d) -> p m d", m=MC)
        kbT = [kT, RB[:, 0:2 * DM].rearrange("p (c n) -> p c n", c=KC)]
        skeys = KV[:, 0:2 * DM].rearrange("p (i k) -> p i k", i=2 * PH)
        skT = KV[:, 2 * DM:4 * DM].rearrange("p (i n) -> p i n", i=2 * PH)
        NZ = CW - 1 + SEQ
        z = TMP[:, 0:NZ]
        zs = TMP[:, NZ:NZ + NSEQ * 10].rearrange("p (b n) -> p b n", b=NSEQ)
        tmp = TMP[:, 594:594 + NT]
        cs = [TMP[:, 1170:1170 + NT], TMP[:, 1746:1746 + NT]]
        zlo = TMP[0:2 + 2 * NSEQ, 1170:1170 + DM]
        ptS = TMP[:, 0:8 * NS].rearrange("p (i n) -> p i n", i=8)
        ffn_g = TMP[:, 1170:1170 + DM]
        qp = [TMP[:, i * 2 * NT:(i + 1) * 2 * NT].rearrange("p (a n) -> p a n", a=2) for i in range(2)]
        Sf = RH[:, 0:2 * DM]
        Tf = RH[:, 2 * DM:3 * DM]
        acc = RH[:, 3 * DM:4 * DM]
        onehot = TMP[:, 0:2 * DM]
        urow = W[:, 0:GRP * DM].rearrange("p (j d) -> p j d", j=GRP)
        vrow = W[:, GRP * DM:2 * GRP * DM].rearrange("p (j d) -> p j d", j=GRP)

        def slot(u):
            s = UNIT[u] % SLOTS
            return W[:, s * UF:(s + 1) * UF].rearrange("p (k n) -> p k n", k=KC)

        def cache_slot(u):
            s = UNIT[u] % SLOTS
            return W[:, s * UF:(s + 1) * UF].rearrange("p (m d) -> p m d", m=MC)

        def pf(job):
            return ps[:, 2 * PAIR[job]:2 * PAIR[job] + 2, 0:HALF]

        def pt(job, rows=P):
            return ps[0:rows, 2 * PAIR[job]:2 * PAIR[job] + 2, :].rearrange("p a n -> p (a n)")

        def halves(ap):
            return ap.rearrange("p (a n) -> p a n", a=2)

        job_done = sem("job_done")
        act_evac = sem("act_evac")
        dve_evac = sem("dve_evac")
        unit_in = [sem(f"unit_in{i}") for i in range(SLOTS)]
        act_chain = sem("act_chain")
        dve_chain = sem("dve_chain")
        topk_step = sem("topk_step")
        pool_chain = sem("pool_chain")
        pool_passed = sem("pool_passed")
        dve_passed = sem("dve_passed")
        setup_in = sem("setup_in")
        par_in = sem("par_in")
        gat_in = sem("gat_in")
        st_in = sem("st_in")
        ln_in = sem("ln_in")
        sgb_in = sem("sgb_in")
        sg8_rep = sem("sg8_rep")
        sq_done = sem("sq_done")
        xn_done = sem("xn_done")
        ln_stat = sem("ln_stat")
        ln_std = sem("ln_std")
        vn_done = sem("vn_done")
        zl_done = sem("zl_done")
        zlo_out = sem("zlo_out")
        vn_out = sem("vn_out")
        mem_in = sem("mem_in")
        mem_norm = sem("mem_norm")
        k_out = sem("k_out")
        v_out = sem("v_out")
        qzero = sem("qzero")
        qm_done = sem("qm_done")
        max_done = sem("max_done")
        exp_done = sem("exp_done")
        prob_done = sem("prob_done")
        ffn_in = sem("ffn_in")
        skeys_in = sem("skeys_in")
        tile_in = sem("tile_in")
        tile_free = sem("tile_free")
        gexp_in = sem("gexp_in")
        gexp_out = sem("gexp_out")
        idx_done = sem("idx_done")
        idxg_free = sem("idxg_free")
        u_in = [sem(f"u_in{j}") for j in range(GRP)]
        v_in = [sem(f"v_in{j}") for j in range(GRP)]
        u_free = sem("u_free")
        v_free = sem("v_free")
        dots_done = sem("dots_done")
        gel_done = sem("gel_done")
        acc_step = sem("acc_step")
        y_done = sem("y_done")
        y_out = sem("y_out")

        class Chain:

            def __init__(self, eng, s, base=0):
                self.eng, self.s, self.n, self.base = eng, s, 0, base

            def link(self, ins):
                self.n += 1
                ins.then_inc(self.s, 1)
                self.eng.wait_ge(self.s, self.base + self.n)

            def mark(self, ins):
                self.n += 1
                ins.then_inc(self.s, 1)

            def wait(self):
                self.eng.wait_ge(self.s, self.base + self.n)

        def await_job(eng, name):
            eng.wait_ge(job_done, JOB[name] + 1)

        def await_evac(eng, name):
            eng.wait_ge(act_evac if owner[name] == "act" else dve_evac, TURN[name])

        with nc.Block() as block:
            @block.sync
            def _(sp):
                sp.dma_start(X[:, 0:4, :], A["x_prompt"][0].rearrange("(t p) d -> p t d", p=P)).then_inc(setup_in, 16)
                sp.dma_start(X[0:NS, 4, :], A["x_sample"].rearrange("b l d -> (b l) d")).then_inc(setup_in, 16)
                sp.wait_ge(setup_in, 32)

            @block.gpsimd
            def _(pool):
                ch = Chain(pool, pool_chain)
                ch.mark(pool.memset(ident[:, :], 0.0))
                ch.mark(pool.memset(tri[:, :], 1.0))
                ch.mark(pool.memset(tri64[:, :], 1.0))
                ch.mark(pool.iota(iota_i[:, :], pattern=[[1, TOPK]], base=0, channel_multiplier=0))
                ch.wait()
                ch.mark(pool.affine_select(out=ident[:, :], in_=ident[:, :], compare_op=ALU.not_equal, fill=1.0,
                                           base=0, pattern=[[-1, P]], channel_multiplier=1))
                ch.mark(pool.affine_select(out=tri[:, :], in_=tri[:, :], compare_op=ALU.is_ge, fill=0.0,
                                           base=0, pattern=[[1, P]], channel_multiplier=-1))
                t64 = tri64[:, :].rearrange("p (b t) -> p b t", b=NSEQ)
                ch.link(pool.affine_select(out=t64, in_=t64, compare_op=ALU.is_ge, fill=0.0,
                                           base=0, pattern=[[8, 8], [1, 8]], channel_multiplier=-1))
                ch.link(pool.affine_select(out=t64, in_=t64, compare_op=ALU.is_ge, fill=0.0,
                                           base=0, pattern=[[-8, 8], [0, 8]], channel_multiplier=1))
                ch.link(pool.tensor_copy(iota16[:, :], iota_i[:, :]))

            @block.vector
            def _(dve):
                ch = Chain(dve, dve_chain)
                ch.mark(dve.memset(eps[:, :], EPS))
                ch.mark(dve.memset(row0[:, :], 0.0))
                ch.mark(dve.memset(ssq[:, :], 1.0))
                ch.mark(dve.memset(std[:, :], 1.0))
                ch.mark(dve.memset(bna[:, :, :], 1.0))
                ch.wait()

        def clear_all():
            with nc.Block() as block:
                @block.gpsimd
                def _(pool):
                    pool.dma_reset()
                    for s in sems:
                        pool.sem_clear(s)

        clear_all()

        def bcast_row(ap):
            return ap.partition_broadcast(P)

        with nc.Fori(0, DEPTH) as l:
            def at(name):
                a = A[name]
                rest = " ".join("abcdef"[:len(a.shape) - 1])
                return a[bass.ds(l, 1)].rearrange(f"z a {rest[2:]} -> (z a) {rest[2:]}".strip())

            def out_at(name):
                a = O[name]
                rest = " ".join("abcdef"[:len(a.shape) - 1])
                return a[bass.ds(l, 1)].rearrange(f"z a {rest[2:]} -> (z a) {rest[2:]}".strip())

            with nc.Block() as block:
                @block.sync
                def _(sp):
                    for i, g in enumerate(("g_mix", "g_xattn", "g_mem")):
                        sp.dma_start(PAR[i * KC:(i + 1) * KC, :],
                                     at(g).rearrange("(c p) -> c p", p=P)).then_inc(par_in, 16)
                    sp.dma_start(PAR[3 * KC:6 * KC, :],
                                 at("conv_w").rearrange("j (c p) -> (j c) p", p=P)).then_inc(par_in, 16)
                    sp.dma_start(state, at("state_conv").rearrange("b j d -> (b j) d")).then_inc(st_in, 16)
                    sp.dma_start(sgw, at("sg_w").rearrange("g t s -> t g s")).then_inc(gat_in, 16)
                    for b in range(NSEQ):
                        sp.dma_start(sgw8[b * NDEC:(b + 1) * NDEC, :, :],
                                     at("sg_w")[:, 0:NDEC, 0:NDEC].rearrange("g t s -> t g s")).then_inc(gat_in, 16)
                    sp.dma_start(ln_g, bcast_row(at("sg_ln_g"))).then_inc(ln_in, 16)
                    sp.dma_start(ln_b, bcast_row(at("sg_ln_b"))).then_inc(ln_in, 16)
                    sp.dma_start(sg_b, at("sg_b").partition_broadcast(P)).then_inc(sgb_in, 16)

                    def store_vn():
                        sp.wait_ge(vn_done, NTILE)
                        sp.dma_start(out_at("new_sg_v_s").rearrange("b l d -> (b l) d"),
                                     VT[0:NS, 4, :]).then_inc(vn_out, 16)

                    def store_conv():
                        await_evac(sp, "zo")
                        sp.dma_start(out_at("new_state_conv_p").rearrange("b j d -> (b j) d"),
                                     zlo[0:2, :]).then_inc(zlo_out, 16)
                        sp.dma_start(out_at("new_state_conv_s").rearrange("b j d -> (b j) d"),
                                     zlo[2:2 + 2 * NSEQ, :]).then_inc(zlo_out, 16)

                    def load_memory():
                        await_evac(sp, ("ob", KC - 1))
                        sp.dma_start(mem, A["mem_prompt"][0].rearrange("(m p) d -> p m d", p=P)).then_inc(mem_in, 16)
                        sp.dma_start(ffn_g, bcast_row(at("g_ffn"))).then_inc(ffn_in, 16)

                    def store_rows(kind, src, name, s):
                        def store():
                            for m in range(MC):
                                await_evac(sp, (kind, m))
                                sp.dma_start(out_at(name)[0, m * P:(m + 1) * P].rearrange("p h e -> p (h e)"),
                                             src[:, m, :]).then_inc(s, 16)
                        return store

                    asides = [("zo", store_vn), ("zo", store_conv), (("ob", KC - 1), load_memory),
                              (("k", MC - 1), store_rows("k", ktok, "new_mem_k_p", k_out)),
                              (("vv", MC - 1), store_rows("vv", vmem, "new_mem_v_p", v_out))]
                    cols = {"c": ("w_in", 1), "h": ("w_in", 2), "b": ("w_in", 0), "u": ("w_in", 3), "v": ("w_in", 4),
                            "ga": ("w_in", 5), "gb": ("w_in", 6), "oa": ("w_a_out", 0), "ob": ("w_b_out", 0),
                            "mo": ("w_mix_o", 0), "k": ("w_xk", 0), "vv": ("w_xv", 0), "q": ("w_xq", 0),
                            "xo": ("w_xo", 0), "pq": ("w_pq", 0)}
                    for i, (kind, n) in enumerate(units):
                        if i >= SLOTS:
                            while asides and JOB[asides[0][0]] < unit_last[i - SLOTS]:
                                await_job(sp, asides[0][0])
                                asides.pop(0)[1]()
                            sp.wait_ge(job_done, unit_last[i - SLOTS] + 1)
                        if kind in ("kb", "vb"):
                            cache = at("cache_mem_k" if kind == "kb" else "cache_mem_v")
                            src = cache[n].rearrange("(m p) h e -> p m (h e)", p=P)
                            dst = cache_slot((kind, n))
                        else:
                            name, part = cols[kind]
                            c0 = part * DM + n * UW
                            src = at(name)[:, c0:c0 + UW].rearrange("(k p) n -> p k n", p=P)
                            dst = slot((kind, n))
                        sp.dma_start(dst, src).then_inc(unit_in[i % SLOTS], 16)
                    assert not asides
                    for s, n in ((vn_out, 1), (zlo_out, 2), (k_out, 2), (v_out, 2)):
                        sp.wait_ge(s, 16 * n)

                @block.gpsimd
                def _(pool):
                    await_job(pool, ("q", KC - 1))
                    pool.memset(RH[:, :], 0.0).then_inc(qzero, 1)
                    await_job(pool, "ss")
                    pool.dma_start(skeys, at("sub_keys").rearrange("h i n k -> n (h i) k")).then_inc(skeys_in, 16)
                    def gather_tile(t, rows):
                        await_job(pool, ("sc", PH - 1, 1))
                        pool.wait_ge(idx_done, t + 1)
                        pool.sem_inc(pool_passed, 1)
                        with pool.Fori(0, NGRP) as k:
                            g = t * NGRP + k
                            pool.wait_ge(idxg_free, g + 1)
                            pool.tensor_copy(idxg[0:rows, :], idx[0:rows, bass.ds(k * GRP, GRP)]).then_inc(pool_chain, 1)
                            pool.wait_ge(pool_chain, g + 1)
                            for name, ring, free, landed in (("peer_u", urow, u_free, u_in), ("peer_v", vrow, v_free, v_in)):
                                table = A[name].rearrange("l n d -> (l n) d")
                                for j in range(GRP):
                                    pool.wait_ge(free, g * GRP + j + 1)
                                    pool.sem_inc(pool_passed, 1)
                                    pool.indirect_dma_start(
                                        ring[0:rows, j, :], None, table,
                                        bass.IndirectOffsetOnAxis(ap=idxg[0:rows, j:j + 1], axis=0)).then_inc(landed[j], 16)

                    with pool.Fori(0, 4) as t:
                        gather_tile(t, P)
                    gather_tile(4, NS)

                @block.tensor
                def _(pe):
                    started = []

                    def begin(name):
                        assert jobs[len(started)][0] == name, (jobs[len(started)], name)
                        started.append(name)
                        if BEFORE[name] is not None:
                            await_evac(pe, BEFORE[name])

                    def end(ins):
                        ins.then_inc(job_done, 1)

                    def await_unit(u):
                        i = UNIT[u]
                        pe.wait_ge(unit_in[i % SLOTS], 16 * (i // SLOTS + 1))

                    def transposes(name, ins, rows_in, cols):
                        begin(name)
                        out = pt(name)
                        step = P if cols == P and rows_in != 2 * NSEQ else None
                        for i, a in enumerate(ins):
                            w = step or rows_in
                            m = pe.transpose(out[0:cols, i * w:i * w + rows_in], a, ident[0:rows_in, 0:rows_in])
                        end(m)

                    def project(name, kind, c, src, fresh=True):
                        begin(name)
                        if c % 2 == 0:
                            await_unit((kind, c // 2))
                        w = slot((kind, c // 2))
                        for k in range(KC):
                            for a in range(2):
                                m = pe.matmul(ps[:, 2 * PAIR[name] + a, 0:HALF], w[:, k, (c % 2) * P:(c % 2) * P + P],
                                              src[:, k, a * HALF:(a + 1) * HALF], start=(k == 0), stop=(k == KC - 1))
                        end(m)

                    def project_tokens(name, kind, src, col, rows, first):
                        begin(name)
                        for a in range(2):
                            for i in range(2):
                                u = (kind, 2 * a + i)
                                if first:
                                    await_unit(u)
                                for k in range(KC):
                                    m = pe.matmul(ps[0:rows, 2 * PAIR[name] + a, i * UW:(i + 1) * UW],
                                                  src[:, k, col:col + rows], slot(u)[:, k, :],
                                                  start=(k == 0), stop=(k == KC - 1))
                        end(m)

                    def norm_transposes(n):
                        for t, rows in TILES:
                            pe.wait_ge(xn_done, n * NTILE + t + 1)
                            transposes(("n", n, t), [XN[0:rows, t, c * P:(c + 1) * P] for c in range(KC)], rows, P)

                    pe.wait_ge(par_in, 64)
                    transposes("par", [PAR[:, :]], 6 * KC, P)
                    pe.wait_ge(st_in, 16)
                    transposes("st", [state[:, c * P:(c + 1) * P] for c in range(KC)], 2 * NSEQ, P)
                    pe.wait_ge(gat_in, 16 * (1 + NSEQ))
                    transposes("sw", [sgw[:, g, :] for g in range(KC)], P, P)
                    pe.wait_ge(sg8_rep, 1)
                    begin("sw64")
                    for g in range(KC):
                        m = pe.transpose(pt("sw64")[0:NS, g * NS:(g + 1) * NS], sgw64[:, g, :], ident[0:NS, 0:NS])
                    end(m)
                    norm_transposes(0)
                    await_evac(pe, ("n", 0, NTILE - 1))
                    for t, rows in TILES:
                        project_tokens(("v", t), "v", hT, t * P, rows, t == 0)
                    for c in range(KC):
                        for kind in "chbu":
                            project((kind, c), kind, c, hT)
                    pe.wait_ge(zl_done, KC)
                    begin("zo")
                    for c in range(KC):
                        m = pe.transpose(pt("zo")[0:2 + 2 * NSEQ, c * P:(c + 1) * P], zl[:, c, :], ident[:, :])
                    end(m)
                    await_evac(pe, "sw64")
                    pe.wait_ge(vn_done, NTILE)
                    for g in range(KC):
                        begin(("mx", g))
                        bank = 2 * PAIR["mx", g]
                        for t in range(4):
                            pe.matmul(ps[:, bank, t * P:(t + 1) * P], VT[:, t, g * P:(g + 1) * P], sgT[:, g, :],
                                      start=True, stop=True)
                        end(pe.matmul(ps[:, bank + 1, 0:NS], VT[0:NS, 4, g * P:(g + 1) * P], sgT64[:, g, :],
                                      start=True, stop=True))
                    await_evac(pe, ("mx", KC - 1))
                    for c in range(KC):
                        project(("ga", c), "ga", c, hT)
                        project(("oa", c), "oa", c, F1)
                        project(("gb", c), "gb", c, hT)
                        project(("ob", c), "ob", c, F2)
                    await_evac(pe, ("ob", KC - 1))
                    for t, rows in TILES:
                        project_tokens(("mo", t), "mo", mT, t * P, rows, t == 0)
                    pe.wait_ge(mem_norm, 1)
                    for m in range(MC):
                        transposes(("mt", m), [mem[:, m, c * P:(c + 1) * P] for c in range(KC)], P, P)
                    await_evac(pe, ("mt", MC - 1))
                    for m in range(MC):
                        project_tokens(("k", m), "k", memT, m * P, P, m == 0)
                    for m in range(MC):
                        project_tokens(("vv", m), "vv", memT, m * P, P, m == 0)
                    await_evac(pe, ("k", MC - 1))
                    for m in range(MC):
                        transposes(("kt", m), [ktok[:, m, c * P:(c + 1) * P] for c in range(KC)], P, P)
                    norm_transposes(1)
                    await_evac(pe, ("n", 1, NTILE - 1))
                    for c in range(KC):
                        project(("q", c), "q", c, hT)
                    await_evac(pe, ("q", KC - 1))

                    def prompt_scores(t):
                        begin(("s", t))
                        for h in range(HEADS):
                            for e in range(2):
                                m = pe.matmul(pt(("s", t))[:, h * NMEM:(h + 1) * NMEM],
                                              qT[:, 2 * h + e, t * P:(t + 1) * P], kT[:, 2 * h + e, :],
                                              start=(e == 0), stop=(e == 1))
                        end(m)

                    def prob_transposes(t, rows):
                        pe.wait_ge(prob_done, t + 1)
                        transposes(("pt", t), [probs[t % 2][0:rows, i * P:(i + 1) * P] for i in range(8)], rows, P)

                    def key_transposes(b):
                        await_unit(("kb", b))
                        for m in range(MC):
                            transposes(("kb", b, m), [cache_slot(("kb", b))[:, m, c * P:(c + 1) * P] for c in range(KC)], P, P)

                    def sample_scores(b):
                        for m in range(MC):
                            await_evac(pe, ("kb", b, m))
                        for h in range(HEADS):
                            for e in range(2):
                                m = pe.matmul(pt("ss", NS)[:, h * NMEM:(h + 1) * NMEM],
                                              qmask[:, 2 * h + e, b * NS:(b + 1) * NS], kbT[b % 2][:, 2 * h + e, :],
                                              start=(b == 0 and e == 0 and h % 2 == 0), stop=(b == NSEQ - 1 and e == 1),
                                              skip_group_check=True)
                        return m

                    for t in range(4):
                        prompt_scores(t)
                        if t:
                            prob_transposes(t - 1, P)
                    key_transposes(0)
                    prob_transposes(3, P)
                    pe.wait_ge(qm_done, 1)
                    held = BEFORE["ss"]
                    await_evac(pe, held)
                    for b in range(1, NSEQ):
                        key_transposes(b)
                        sample_scores(b - 1)
                    begin("ss")
                    end(sample_scores(NSEQ - 1))
                    for c in range(KC):
                        begin(("o", c))
                        if c == 0:
                            await_evac(pe, ("pt", 3))
                        for m in range(MC):
                            last = pe.matmul(ps[:, 2 * PAIR["o", c], :], vmem[:, m, c * P:(c + 1) * P],
                                             PT[:, (c // 2) * 2 + m, :], start=(m == 0), stop=(m == MC - 1))
                        end(last)
                    prob_transposes(4, NS)
                    begin("os")
                    await_evac(pe, ("pt", 4))
                    for b in range(NSEQ):
                        await_unit(("vb", b))
                        for c in range(KC):
                            for m in range(MC):
                                col = c * NS + b * NDEC
                                last = pe.matmul(pt("os")[:, col:col + NDEC],
                                                 cache_slot(("vb", b))[:, m, c * P:(c + 1) * P],
                                                 ptS[:, (c // 2) * 2 + m, b * NDEC:(b + 1) * NDEC],
                                                 start=(m == 0), stop=(m == MC - 1))
                    end(last)
                    await_evac(pe, ("o", KC - 1))
                    await_evac(pe, "os")
                    for t, rows in TILES:
                        project_tokens(("xo", t), "xo", oT, t * P, rows, t == 0)
                    pe.wait_ge(skeys_in, 16)
                    for i in range(2):
                        transposes(f"sk{i}", [skeys[:, 8 * i + j, :] for j in range(8)], P, P)
                    norm_transposes(2)
                    await_evac(pe, ("n", 2, NTILE - 1))
                    for c in range(2):
                        project(("pq", c), "pq", c, hT)
                    for h in range(PH):
                        if h + 1 < PH:
                            for c in (2 * h + 2, 2 * h + 3):
                                project(("pq", c), "pq", c, hT)
                        begin(("sc", h, 0))
                        await_evac(pe, ("pq", 2 * h + 1))
                        for t in range(4):
                            for i in range(2):
                                m = pe.matmul(pt(("sc", h, 0))[:, t * 256 + i * P:t * 256 + (i + 1) * P],
                                              qp[h % 2][:, i, t * P:(t + 1) * P], skT[:, 2 * h + i, :],
                                              start=True, stop=True)
                        end(m)
                        begin(("sc", h, 1))
                        for i in range(2):
                            m = pe.matmul(pt(("sc", h, 1), NS)[:, i * P:(i + 1) * P],
                                          qp[h % 2][:, i, SEQ:NT], skT[:, 2 * h + i, :], start=True, stop=True)
                        end(m)
                    assert len(started) == len(jobs)

                @block.scalar
                def _(act):
                    ch = Chain(act, act_chain)
                    seen = []

                    def take(name):
                        mine = [n for n, o in jobs if o == "act"]
                        assert mine[len(seen)] == name, (mine[len(seen)], name)
                        seen.append(name)
                        await_job(act, name)

                    def evac(name, out, in_, func=ACT.Copy):
                        take(name)
                        act.activation(out, in_, func).then_inc(act_evac, 1)

                    def squares(n):
                        for t, rows in TILES:
                            if n:
                                await_evac(act, ("mo" if n == 1 else "xo", t))
                            if n == 1 and t == 0:
                                await_job(act, ("mo", NTILE - 1))
                            ch.mark(act.activation(XN[0:rows, t, :], X[0:rows, t, :], ACT.Square,
                                                   accum_out=ssq[0:rows, t:t + 1]))
                        ch.wait()
                        act.activation(std[:, 0:NTILE], ssq[:, 0:NTILE], ACT.Sqrt, bias=eps[:, :],
                                       scale=1.0 / DM).then_inc(sq_done, 1)

                    evac("par", PARC[:, :], pt("par")[:, 0:6 * KC])
                    evac("st", stT[:, :, :], pt("st")[:, 0:KC * 2 * NSEQ].rearrange("p (c r) -> p c r", c=KC))
                    squares(0)
                    for t, rows in TILES:
                        take(("v", t))
                        if t == 0:
                            await_job(act, ("n", 0, NTILE - 1))
                        act.activation(VT[0:rows, t, :], pt(("v", t), rows), ACT.Gelu_apprx_tanh).then_inc(act_evac, 1)
                    act.wait_ge(ln_stat, NTILE)
                    act.activation(std[:, 0:NTILE], bna[:, :, 1], ACT.Sqrt, bias=eps[:, :]).then_inc(ln_std, 1)
                    for c in range(KC):
                        if c >= 2:
                            await_evac(act, ("h", c - 2))
                        evac(("c", c), halves(cs[c % 2]), pf(("c", c)))
                        evac(("u", c), halves(F2[:, c, :]), pf(("u", c)), ACT.Gelu_apprx_tanh)
                    await_evac(act, ("h", KC - 1))
                    take("zo")
                    act.activation(zlo, pt("zo", 2 + 2 * NSEQ), ACT.Copy).then_inc(act_evac, 1)
                    act.wait_ge(zlo_out, 32)
                    for c in range(KC):
                        if c:
                            await_evac(act, ("oa", c - 1))
                        evac(("ga", c), halves(cs[0]), pf(("ga", c)), ACT.Sigmoid)
                        if c:
                            await_evac(act, ("ob", c - 1))
                        evac(("gb", c), halves(cs[1]), pf(("gb", c)), ACT.Sigmoid)
                    act.wait_ge(mem_in, 16)
                    for m in range(MC):
                        ch.mark(act.activation(memT.rearrange("p c n -> p (c n)")[:, m * DM:(m + 1) * DM], mem[:, m, :],
                                               ACT.Square, accum_out=ssq[:, 5 + m:6 + m]))
                    ch.wait()
                    act.activation(std[:, 5:7], ssq[:, 5:7], ACT.Sqrt, bias=eps[:, :], scale=1.0 / DM).then_inc(sq_done, 1)
                    squares(1)
                    for m in range(MC):
                        evac(("k", m), ktok[:, m, :], pt(("k", m)))
                    for m in range(MC):
                        evac(("vv", m), vmem[:, m, :], pt(("vv", m)))
                    for c in range(KC):
                        evac(("q", c), halves(qT[:, c, :]), pf(("q", c)))

                    def exps(t, rows, name):
                        take(name)
                        act.wait_ge(max_done, t + 1)
                        if t >= 2:
                            await_job(act, ("pt", t - 2))
                        for h in range(HEADS):
                            e = act.activation(probs[t % 2][0:rows, h * NMEM:(h + 1) * NMEM],
                                               pt(name, rows)[:, h * NMEM:(h + 1) * NMEM], ACT.Exp,
                                               bias=nmax[0:rows, t, h:h + 1], scale=1.0 / 16.0,
                                               accum_out=rsum[0:rows, t, h:h + 1])
                        e.then_inc(act_evac, 1)

                    def evac_probs(t):
                        evac(("pt", t), PT[:, :, t * P:(t + 1) * P],
                             pt(("pt", t)).rearrange("p (i n) -> p i n", i=8))

                    def evac_keys(b):
                        evac(("kb", b, 0), kbT[b % 2][:, :, 0:P], pt(("kb", b, 0)).rearrange("p (c n) -> p c n", c=KC))

                    for t in range(4):
                        exps(t, P, ("s", t))
                        if t:
                            evac_probs(t - 1)
                    evac_keys(0)
                    evac_probs(3)
                    act.wait_ge(qm_done, 1)
                    for b in range(1, NSEQ):
                        evac_keys(b)
                    exps(4, NS, "ss")
                    act.wait_ge(k_out, 32)
                    for c in range(KC):
                        evac(("o", c), oT[:, c, 0:SEQ], ps[:, 2 * PAIR["o", c], :])
                    evac(("pt", 4), ptS, pt(("pt", 4)).rearrange("p (i n) -> p i n", i=8)[:, :, 0:NS])
                    squares(2)
                    for h in range(PH):
                        lo = 0 if h == 0 else 2 * h + 2
                        for c in range(lo, min(2 * h + 4, 2 * PH)):
                            evac(("pq", c), halves(qp[c // 2 % 2][:, c % 2, :]), pf(("pq", c)))
                        evac(("sc", h, 0), S[:, 0:4, h * 256:(h + 1) * 256],
                             pt(("sc", h, 0)).rearrange("p (t n) -> p t n", t=4))
                        evac(("sc", h, 1), S[0:NS, 4, h * 256:(h + 1) * 256], pt(("sc", h, 1), NS)[:, 0:256])
                    assert len(seen) == sum(o == "act" for _, o in jobs)
                    act.wait_ge(act_evac, TURN["sc", PH - 1, 1])

                    def peer_tile(t, rows):
                        act.wait_ge(tile_free, t + 1)
                        act.activation(Sf[0:rows, :], S[0:rows, bass.ds(t, 1), :].rearrange("p a n -> p (a n)"), ACT.Copy).then_inc(tile_in, 1)
                        act.activation(Tf[0:rows, :], XN[0:rows, bass.ds(t, 1), :].rearrange("p a n -> p (a n)"), ACT.Copy).then_inc(tile_in, 1)
                        act.wait_ge(gexp_in, t + 1)
                        act.activation(tops[0:rows, :, :], tops[0:rows, :, :], ACT.Exp).then_inc(gexp_out, 1)
                        with act.Fori(0, NGRP) as k:
                            act.wait_ge(dots_done, t * NGRP + k + 1)
                            act.activation(gel[0:rows, :], dots[0:rows, :], ACT.Gelu_apprx_tanh).then_inc(gel_done, 1)

                    with act.Fori(0, 4) as t:
                        peer_tile(t, P)
                    peer_tile(4, NS)

                @block.vector
                def _(dve):
                    ch = Chain(dve, dve_chain)
                    seen = []

                    def take(name):
                        mine = [n for n, o in jobs if o == "dve"]
                        assert mine[len(seen)] == name, (mine[len(seen)], name)
                        seen.append(name)
                        await_job(dve, name)

                    def done(ins):
                        ins.then_inc(dve_evac, 1)

                    def gain(i):
                        return PARC[:, i * KC:(i + 1) * KC]

                    def reciprocals(wait, n, a, b):
                        dve.wait_ge(wait, n)
                        ch.link(dve.reciprocal(rstd[:, a:b], std[:, a:b]))

                    def norm(n, wait_n):
                        reciprocals(sq_done, wait_n, 0, NTILE)
                        for t, rows in TILES:
                            if n == 2:
                                if t == 0:
                                    dve.wait_ge(ffn_in, 16)
                                ins = dve.scalar_tensor_tensor(out=XN[0:rows, t, :], in0=X[0:rows, t, :],
                                                               scalar=rstd[0:rows, t:t + 1], in1=ffn_g[0:rows, :],
                                                               op0=ALU.mult, op1=ALU.mult)
                            else:
                                ins = dve.tensor_scalar(XN[0:rows, t, :], X[0:rows, t, :], rstd[0:rows, t:t + 1], None, ALU.mult)
                            ins.then_inc(xn_done, 1)
                        for t, rows in TILES:
                            take(("n", n, t))
                            src = pt(("n", n, t)).rearrange("p (c n) -> p c n", c=KC)[:, :, 0:rows]
                            dst = hT[:, :, t * P:t * P + rows]
                            if n == 2:
                                done(dve.tensor_copy(dst, src))
                            else:
                                done(dve.tensor_tensor(dst, src, gain(n).unsqueeze(2).to_broadcast([P, KC, rows]), ALU.mult))

                    dve.wait_ge(gat_in, 16 * (1 + NSEQ))
                    s64 = sgw64.rearrange("p g (b s) -> p g b s", b=NSEQ)
                    for g in range(KC):
                        r = dve.tensor_copy(s64[:, g], sgw8[:, g, :].unsqueeze(1).to_broadcast([NS, NSEQ, NDEC]))
                    r.then_inc(sg8_rep, 1)
                    take("sw")
                    done(dve.tensor_tensor(sgT, pt("sw").rearrange("p (g t) -> p g t", g=KC),
                                           tri[:, :].unsqueeze(1).to_broadcast([P, KC, P]), ALU.mult))
                    take("sw64")
                    done(dve.tensor_tensor(sgT64, pt("sw64", NS)[:, 0:8 * NS].rearrange("p (g t) -> p g t", g=KC),
                                           tri64[:, :].unsqueeze(1).to_broadcast([NS, KC, NS]), ALU.mult))
                    await_evac(dve, "par")
                    norm(0, 1)
                    for t, rows in TILES:
                        await_evac(dve, ("v", t))
                        for i in range(2):
                            ch.mark(dve.bn_stats(bns[0:rows, t, i, :], VT[0:rows, t, i * 512:(i + 1) * 512]))
                        ch.wait()
                        dve.bn_aggr(bna[0:rows, t, :], bns[0:rows, t, :, :]).then_inc(ln_stat, 1)
                    reciprocals(ln_std, 1, 0, NTILE)
                    dve.wait_ge(ln_in, 32)
                    for t, rows in TILES:
                        v = VT[0:rows, t, :]
                        ch.link(dve.tensor_scalar(v, v, bna[0:rows, t, 0:1], rstd[0:rows, t:t + 1], ALU.subtract, ALU.mult))
                        ch.link(dve.tensor_tensor(v, v, ln_g[0:rows, :], ALU.mult))
                        dve.tensor_tensor(v, v, ln_b[0:rows, :], ALU.add).then_inc(vn_done, 1)
                    ch.mark(dve.memset(z[:, 0:CW - 1], 0.0))
                    ts = tmp[:, SEQ:NT].rearrange("p (b n) -> p b n", b=NSEQ)
                    for c in range(KC):
                        def tap(j):
                            i = 3 * KC + j * KC + c
                            return PARC[:, i:i + 1]
                        await_evac(dve, ("c", c))
                        take(("h", c))
                        b0 = 2 * PAIR["h", c]
                        src = cs[c % 2]
                        ch.mark(dve.tensor_tensor(z[:, 2:2 + HALF], ps[:, b0, 0:HALF], src[:, 0:HALF], ALU.mult))
                        ch.mark(dve.tensor_tensor(z[:, 2 + HALF:NZ], ps[:, b0 + 1, 0:SEQ - HALF], src[:, HALF:SEQ], ALU.mult))
                        done(dve.tensor_tensor(zs[:, :, 2:10], ps[:, b0 + 1, SEQ - HALF:HALF].rearrange("p (b n) -> p b n", b=NSEQ),
                                               src[:, SEQ:NT].rearrange("p (b n) -> p b n", b=NSEQ), ALU.mult))
                        ch.mark(dve.tensor_copy(zs[:, :, 0:2], stT[:, c, :].rearrange("p (b j) -> p b j", b=NSEQ)))
                        ch.wait()
                        ch.mark(dve.tensor_copy(zl[:, c, 0:2], z[:, SEQ:NZ]))
                        dve.tensor_copy(zl[:, c, 2:2 + 2 * NSEQ].rearrange("p (b j) -> p b j", b=NSEQ), zs[:, :, 8:10]).then_inc(zl_done, 1)
                        ch.mark(dve.tensor_scalar(tmp[:, 0:SEQ], z[:, 0:SEQ], tap(0), None, ALU.mult))
                        ch.mark(dve.tensor_scalar(ts, zs[:, :, 0:8], tap(0), None, ALU.mult))
                        for j in (1, 2):
                            ch.wait()
                            ch.mark(dve.scalar_tensor_tensor(out=tmp[:, 0:SEQ], in0=z[:, j:j + SEQ], scalar=tap(j),
                                                             in1=tmp[:, 0:SEQ], op0=ALU.mult, op1=ALU.add))
                            ch.mark(dve.scalar_tensor_tensor(out=ts, in0=zs[:, :, j:j + 8], scalar=tap(j),
                                                             in1=ts, op0=ALU.mult, op1=ALU.add))
                        ch.wait()
                        take(("b", c))
                        done(dve.tensor_tensor(halves(F1[:, c, :]), pf(("b", c)), halves(tmp), ALU.mult))
                        await_evac(dve, ("b", c))
                    dve.wait_ge(sgb_in, 16)
                    for g in range(KC):
                        take(("mx", g))
                        bank = 2 * PAIR["mx", g]
                        ch.mark(dve.tensor_tensor(tmp[:, 0:SEQ].rearrange("p (t n) -> p t n", t=4),
                                                  ps[:, bank, :].rearrange("p (t n) -> p t n", t=4),
                                                  sg_b[:, g, :].unsqueeze(1).to_broadcast([P, 4, P]), ALU.add))
                        ch.mark(dve.tensor_tensor(ts, ps[:, bank + 1, 0:NS].rearrange("p (b n) -> p b n", b=NSEQ),
                                                  sg_b[:, g, 0:NDEC].unsqueeze(1).to_broadcast([P, NSEQ, NDEC]), ALU.add))
                        ch.wait()
                        await_evac(dve, ("u", g))
                        done(dve.tensor_tensor(F2[:, g, :], F2[:, g, :], tmp, ALU.mult))
                        await_evac(dve, ("mx", g))
                    dve.wait_ge(vn_out, 16)
                    for c in range(KC):
                        await_evac(dve, ("ga", c))
                        take(("oa", c))
                        done(dve.tensor_tensor(halves(mT[:, c, :]), pf(("oa", c)), halves(cs[0]), ALU.mult))
                        await_evac(dve, ("gb", c))
                        take(("ob", c))
                        ch.link(dve.tensor_tensor(halves(tmp), pf(("ob", c)), halves(cs[1]), ALU.mult))
                        done(dve.tensor_tensor(mT[:, c, :], mT[:, c, :], tmp, ALU.add))
                        await_evac(dve, ("ob", c))

                    def add_to_x(kind):
                        for t, rows in TILES:
                            take((kind, t))
                            done(dve.tensor_tensor(X[0:rows, t, :], X[0:rows, t, :], pt((kind, t), rows), ALU.add))

                    add_to_x("mo")
                    reciprocals(sq_done, 2, 5, 7)
                    for m in range(MC):
                        n = dve.tensor_scalar(mem[:, m, :], mem[:, m, :], rstd[:, 5 + m:6 + m], None, ALU.mult)
                    n.then_inc(mem_norm, 1)
                    for m in range(MC):
                        take(("mt", m))
                        done(dve.tensor_tensor(memT[:, :, m * P:(m + 1) * P], pt(("mt", m)).rearrange("p (c n) -> p c n", c=KC),
                                               gain(2).unsqueeze(2).to_broadcast([P, KC, P]), ALU.mult))
                    for m in range(MC):
                        take(("kt", m))
                        done(dve.tensor_copy(kT[:, :, m * P:(m + 1) * P], pt(("kt", m)).rearrange("p (c n) -> p c n", c=KC)))
                    norm(1, 3)

                    def maxima(t, rows, name):
                        await_job(dve, name)
                        ch.link(dve.tensor_reduce(rmax[0:rows, t, :], pt(name, rows).rearrange("p (h m) -> p h m", h=HEADS), AX, ALU.max))
                        dve.tensor_scalar(nmax[0:rows, t, :], rmax[0:rows, t, :], -1.0 / 16.0, None, ALU.mult).then_inc(max_done, 1)

                    def normalise(t, rows, name):
                        await_evac(dve, name)
                        ch.link(dve.reciprocal(rinv[0:rows, t, :], rsum[0:rows, t, :]))
                        pr = probs[t % 2][0:rows, :].rearrange("p (h m) -> p h m", h=HEADS)
                        dve.tensor_tensor(pr, pr, rinv[0:rows, t, :].unsqueeze(2).to_broadcast([rows, HEADS, NMEM]), ALU.mult).then_inc(prob_done, 1)

                    dve.wait_ge(qzero, 1)
                    await_evac(dve, ("q", KC - 1))
                    for c in range(KC):
                        q = dve.tensor_copy(qmask[:, c, :].rearrange("p (b n) -> p b n", n=72)[:, :, 0:NDEC],
                                            qT[:, c, SEQ:NT].rearrange("p (b n) -> p b n", b=NSEQ))
                    q.then_inc(qm_done, 1)
                    for t in range(4):
                        maxima(t, P, ("s", t))
                        if t:
                            normalise(t - 1, P, ("s", t - 1))
                    normalise(3, P, ("s", 3))
                    for b in range(NSEQ):
                        take(("kb", b, 1))
                        done(dve.tensor_copy(kbT[b % 2][:, :, P:2 * P], pt(("kb", b, 1)).rearrange("p (c n) -> p c n", c=KC)))
                    maxima(4, NS, "ss")
                    normalise(4, NS, "ss")
                    take("os")
                    dve.wait_ge(k_out, 32)
                    done(dve.tensor_copy(oT[:, :, SEQ:NT], pt("os")[:, 0:KC * NS].rearrange("p (c n) -> p c n", c=KC)))
                    add_to_x("xo")
                    for i in range(2):
                        take(f"sk{i}")
                        dve.wait_ge(v_out, 32)
                        done(dve.tensor_copy(skT[:, 8 * i:8 * i + 8, :], pt(f"sk{i}").rearrange("p (i n) -> p i n", i=8)))
                    norm(2, 4)
                    assert len(seen) == sum(o == "dve" for _, o in jobs)

                    dve.sem_inc(tile_free, 1)
                    dve.sem_inc(idxg_free, 1)
                    await_job(dve, ("sc", PH - 1, 1))
                    dve.sem_inc(u_free, GRP)
                    dve.sem_inc(v_free, GRP)

                    def peer_tile(t, rows):
                        dve.sem_clear(topk_step)
                        c = Chain(dve, topk_step)
                        r = slice(0, rows)
                        await_job(dve, ("sc", PH - 1, 1))
                        dve.wait_ge(tile_in, 2 * t + 2)
                        dve.sem_inc(dve_passed, 1)
                        part = [Sf[r, i * P:(i + 1) * P] for i in range(2 * PH)]
                        cand = [Sf[r, h * 256:(h + 1) * 256] for h in range(PH)]

                        def top16(src, vals, where):
                            for i, s in enumerate(src):
                                c.mark(dve.max(vals[i][:, 0:8], s))
                            c.wait()
                            for i, s in enumerate(src):
                                c.mark(dve.max_index(where[i][:, 0:8], vals[i][:, 0:8], s))
                            c.wait()
                            for i, s in enumerate(src):
                                c.mark(dve.match_replace(s, vals[i][:, 0:8], s, LOWEST))
                            c.wait()
                            for i, s in enumerate(src):
                                c.mark(dve.max(vals[i][:, 8:16], s))
                            c.wait()
                            for i, s in enumerate(src):
                                c.mark(dve.max_index(where[i][:, 8:16], vals[i][:, 8:16], s))
                            c.wait()

                        top16(part, [m16[r, i, :] for i in range(2 * PH)], [i16[r, i, :] for i in range(2 * PH)])
                        c.mark(dve.tensor_copy(i16f[r, :, :], i16[r, :, :]))
                        mm = m16[r, :, :].rearrange("p (h i) n -> p h i n", i=2)
                        c.link(dve.tensor_tensor(Sf[r, :].rearrange("p (h a b) -> p h a b", h=PH, a=TOPK),
                                                 mm[:, :, 0, :].unsqueeze(3).to_broadcast([rows, PH, TOPK, TOPK]),
                                                 mm[:, :, 1, :].unsqueeze(2).to_broadcast([rows, PH, TOPK, TOPK]), ALU.add))
                        top16(cand, [tops[r, h, :] for h in range(PH)],
                              [pos[r, 0, h * TOPK:(h + 1) * TOPK] for h in range(PH)])
                        c.link(dve.tensor_tensor(gate[r, :].rearrange("p (h n) -> p h n", h=PH), tops[r, :, :],
                                                 tops[r, :, 0:1].to_broadcast([rows, PH, TOPK]), ALU.subtract))
                        dve.tensor_copy(tops[r, :, :], gate[r, :].rearrange("p (h n) -> p h n", h=PH)).then_inc(gexp_in, 1)
                        c.link(dve.tensor_single_scalar(pos[r, 1, :], pos[r, 0, :], 15, ALU.bitwise_and))
                        c.link(dve.tensor_single_scalar(pos[r, 0, :], pos[r, 0, :], 4, ALU.logical_shift_right))
                        c.link(dve.tensor_copy(posf[r, :, :], pos[r, :, :]))
                        ii = i16f[r, :, :].rearrange("p (h i) n -> p h i n", i=2)
                        oh = onehot[r, :].rearrange("p (s j) -> p s j", j=TOPK)
                        oh4 = onehot[r, :].rearrange("p (h s j) -> p h s j", h=PH, j=TOPK)
                        for i in range(2):
                            c.link(dve.tensor_tensor(oh, posf[r, i, :].unsqueeze(2).to_broadcast([rows, NSEL, TOPK]),
                                                     iota16[r, :].unsqueeze(1).to_broadcast([rows, NSEL, TOPK]), ALU.is_equal))
                            c.link(dve.tensor_tensor(oh4, oh4, ii[:, :, i, :].unsqueeze(2).to_broadcast([rows, PH, TOPK, TOPK]), ALU.mult))
                            c.link(dve.tensor_reduce(sel[r, i, :], oh, AX, ALU.add))
                        c.link(dve.scalar_tensor_tensor(out=sel[r, 0, :], in0=sel[r, 0, :], scalar=float(NK), in1=sel[r, 1, :],
                                                        op0=ALU.mult, op1=ALU.add))
                        dve.tensor_scalar(idx[r, :], sel[r, 0, :], row0[r, :], None, ALU.add).then_inc(idx_done, 1)
                        dve.wait_ge(gexp_out, t + 1)
                        c.link(dve.tensor_reduce(gsum[r, :], tops[r, :, :], AX, ALU.add))
                        c.link(dve.reciprocal(ginv[r, :], gsum[r, :]))
                        c.mark(dve.tensor_tensor(gate[r, :].rearrange("p (h n) -> p h n", h=PH), tops[r, :, :],
                                                 ginv[r, :].unsqueeze(2).to_broadcast([rows, PH, TOPK]), ALU.mult))
                        c.link(dve.memset(acc[r, :], 0.0))
                        with dve.Fori(0, NGRP) as k:
                            g = t * NGRP + k
                            for j in range(GRP):
                                dve.wait_ge(u_in[j], g * 16 + 16)
                                dve.tensor_tensor_reduce(urow[r, j, :], urow[r, j, :], Tf[r, :], 1.0, 0.0, ALU.mult, ALU.add,
                                                         dots[r, j:j + 1]).then_inc(u_free, 1)
                            dve.wait_ge(u_free, g * GRP + 2 * GRP)
                            dve.sem_inc(dots_done, 1)
                            dve.wait_ge(gel_done, g + 1)
                            dve.tensor_tensor(wts[r, :], gel[r, :], gate[r, bass.ds(k * GRP, GRP)], ALU.mult).then_inc(acc_step, 1)
                            for j in range(GRP):
                                dve.wait_ge(v_in[j], g * 16 + 16)
                                dve.wait_ge(acc_step, g + 1)
                                dve.wait_ge(v_free, g * GRP + GRP + j)
                                dve.scalar_tensor_tensor(out=acc[r, :], in0=vrow[r, j, :], scalar=wts[r, j:j + 1], in1=acc[r, :],
                                                         op0=ALU.mult, op1=ALU.add).then_inc(v_free, 1)
                            dve.wait_ge(v_free, g * GRP + 2 * GRP)
                            dve.sem_inc(idxg_free, 1)
                        xt = X[r, bass.ds(t, 1), :].rearrange("p a n -> p (a n)")
                        c.link(dve.tensor_tensor(xt, xt, acc[r, :], ALU.add))
                        dve.sem_inc(tile_free, 1)

                    with dve.Fori(0, 4) as t:
                        peer_tile(t, P)
                    peer_tile(4, NS)
                    dve.tensor_scalar(row0[:, :], row0[:, :], float(NE), None, ALU.add)

            clear_all()

        with nc.Block() as block:
            @block.scalar
            def _(act):
                ch = Chain(act, act_chain)
                for t, rows in TILES:
                    ch.mark(act.activation(XN[0:rows, t, :], X[0:rows, t, :], ACT.Square, accum_out=ssq[0:rows, t:t + 1]))
                ch.wait()
                act.activation(std[:, 0:NTILE], ssq[:, 0:NTILE], ACT.Sqrt, bias=eps[:, :], scale=1.0 / DM).then_inc(sq_done, 1)

            @block.vector
            def _(dve):
                dve.wait_ge(sq_done, 1)
                Chain(dve, dve_chain).link(dve.reciprocal(rstd[:, 0:NTILE], std[:, 0:NTILE]))
                dve.wait_ge(ffn_in, 16)
                for t, rows in TILES:
                    dve.scalar_tensor_tensor(out=XN[0:rows, t, :], in0=X[0:rows, t, :], scalar=rstd[0:rows, t:t + 1],
                                             in1=ffn_g[0:rows, :], op0=ALU.mult, op1=ALU.mult).then_inc(y_done, 1)

            @block.sync
            def _(sp):
                sp.dma_start(ffn_g, bcast_row(A["g_final"])).then_inc(ffn_in, 16)
                for t, rows in TILES:
                    sp.wait_ge(y_done, t + 1)
                    dst = O["y_prompt"][0, t * P:(t + 1) * P, :] if t < 4 else O["y_sample"].rearrange("b l d -> (b l) d")
                    sp.dma_start(dst, XN[0:rows, t, :]).then_inc(y_out, 16)
                sp.wait_ge(y_out, 16 * NTILE)


_INS = ["x_prompt", "x_sample", "state_conv", "cache_mem_k", "cache_mem_v", "mem_prompt", "g_mix", "w_in", "conv_w",
        "w_a_out", "sg_ln_g", "sg_ln_b", "sg_w", "sg_b", "w_b_out", "w_mix_o", "g_xattn", "g_mem", "w_xq", "w_xk",
        "w_xv", "w_xo", "g_ffn", "w_pq", "sub_keys", "peer_u", "peer_v", "g_final"]
_OUTS = [("y_prompt", (1, SEQ, DM)), ("y_sample", (NSEQ, NDEC, DM)),
         ("new_state_conv_p", (DEPTH, 1, CW - 1, DM)), ("new_mem_k_p", (DEPTH, 1, NMEM, HEADS, HD)),
         ("new_mem_v_p", (DEPTH, 1, NMEM, HEADS, HD)), ("new_state_conv_s", (DEPTH, NSEQ, CW - 1, DM)),
         ("new_sg_v_s", (DEPTH, NSEQ, NDEC, DM))]


def kernel(**inputs):
    import numpy as _np
    import concourse.bacc as _bacc
    from concourse import mybir as _mybir
    from concourse.bass_utils import run_bass_kernel_spmd as _run

    nc = _bacc.Bacc("TRN2", target_bir_lowering=False, num_devices=1)
    arrays, ins, outs = {}, {}, {}
    for name in _INS:
        a = _np.ascontiguousarray(inputs[name])
        arrays[f"in_{name}_dram"] = a
        ins[name] = nc.dram_tensor(f"in_{name}_dram", a.shape, _mybir.dt.from_np(a.dtype), kind="ExternalInput").ap()
    for name, shape in _OUTS:
        outs[name] = nc.dram_tensor(f"out_{name}_dram", shape, F32, kind="ExternalOutput").ap()
    decoder_step(nc, ins, outs)
    r = _run(nc, [arrays], core_ids=[0])
    return tuple(r.results[0][f"out_{name}_dram"] for name, _ in _OUTS)
```

```python
from contextlib import ExitStack

import concourse.bass as bass
from concourse import mybir

P = 128
DM = 1024
KC = DM // P
SEQ, NSEQ, NDEC = 512, 8, 8
NS = NSEQ * NDEC
GROUPS = [[(0, P), (1, P)], [(2, P), (3, P), (4, NS)]]
GC = 2 * P
NTILE = 5
DEPTH, CW = 2, 3
HEADS, HD, NMEM = 4, 256, 256
MC = NMEM // P
PH, NK, TOPK = 8, 128, 16
NE = NK * NK
NSEL = PH * TOPK
EPS = 1e-6
UW = 256
SLOTS = 6
UF = KC * UW
GRP = 4
TSLOT = 4
LAG = 8
STEPS = 17
GATE_STEP = 15
LOWEST = -3.0e38

F32 = mybir.dt.float32
U32 = mybir.dt.uint32
I32 = mybir.dt.int32
ALU = mybir.AluOpType
ACT = mybir.ActivationFunctionType
AX = mybir.AxisListType.X


def ncols(g):
    return GC + (NS if g else 0)


def tile_groups(rows):
    return NSEL * rows // P // GRP


def pass_groups(p):
    return sum(tile_groups(rows) for t, rows in GROUPS[p % 2])


def phase_jobs(g):
    nt = len(GROUPS[g])
    fm, tm = 8 * ncols(g) * 4 / 2400, 13.7
    jobs = [(("par",), "act", 1, 0.2)]
    if g:
        jobs += [(("st",), "act", 1, 1)]
    jobs += [(("sw",), "dve", 2, 1)]
    if g:
        jobs += [(("sw64",), "dve", 1, 1)]
    jobs += [(("n", 0, i), "dve", 2, 2 if i else 14) for i in range(nt)]
    jobs += [(("v", i), "act", 2, tm) for i in range(nt)]
    for c in range(KC):
        jobs += [(("c", c), "act", 1, fm), (("h", c), "dve", 1, fm), (("b", c), "dve", 1, fm), (("u", c), "act", 1, fm)]
    if g:
        jobs += [(("zo",), "act", 2, 1)]
    jobs += [(("mx", c), "dve", 1, 2.5) for c in range(KC)]
    for c in range(KC):
        jobs += [(("ga", c), "act", 1, fm), (("oa", c), "dve", 1, fm), (("gb", c), "act", 1, fm), (("ob", c), "dve", 1, fm)]
    jobs += [(("mo", i), "dve", 2, tm) for i in range(nt)]
    if not g:
        jobs += [(("mt", m), "dve", 2, 1) for m in range(MC)]
        jobs += [(("k", m), "act", 2, tm) for m in range(MC)]
        jobs += [(("vv", m), "act", 2, tm) for m in range(MC)]
    jobs += [(("kt", m), "dve", 2, 1) for m in range(MC)]
    jobs += [(("n", 1, i), "dve", 2, 2 if i else 14) for i in range(nt)]
    jobs += [(("q", c), "act", 1, fm) for c in range(KC)]
    jobs += [(("s", 0), "act", 2, 4), (("s", 1), "act", 2, 4), (("pt", 0), "act", 2, 6)]
    if g:
        jobs += [(("kb", 0, m), ("act", "dve")[m], 2, 1) for m in range(MC)]
    jobs += [(("pt", 1), "act", 2, 1)]
    if g:
        for b in range(1, NSEQ):
            jobs += [(("kb", b, m), ("act", "dve")[m], 2, 4) for m in range(MC)]
        jobs += [(("ss",), "act", 1, 8), (("sb",), "act", 2, 8)]
    jobs += [(("o", c), "act", 1, 1) for c in range(KC)]
    if g:
        jobs += [(("pt", 2), "act", 2, 10)]
        jobs += [(("os", b), "dve", 1, 2) for b in range(NSEQ)]
    jobs += [(("xo", i), "dve", 2, tm) for i in range(nt)]
    jobs += [(("sk", 0), "dve", 2, 1), (("sk", 1), "dve", 2, 1)]
    jobs += [(("n", 2, i), "dve", 2, 2 if i else 14) for i in range(nt)]
    jobs += [(("pq", 0), "act", 1, fm), (("pq", 1), "act", 1, fm)]
    for h in range(PH):
        if h + 1 < PH:
            jobs += [(("pq", 2 * h + 2), "act", 1, fm), (("pq", 2 * h + 3), "act", 1, fm)]
        jobs += [(("sc", h), "act", 2, 2)]
    return jobs


def plan_jobs():
    jobs, index, bank, before, turn, ahead = [], {}, {}, {}, {}, {}
    user, counts, cursor, done = {}, {"act": 0, "dve": 0}, 0, 0
    for p in range(2 * DEPTH):
        mine = phase_jobs(p % 2)
        total, past = sum(j[3] for j in mine), 0.0
        tiles = len(GROUPS[(p - 1) % 2]) if p else 0
        end = done + pass_groups(p - 1) - LAG if p else 0
        start = done + LAG * (tiles - 1) if p else 0
        names = [j[0] for j in mine]
        for k, (name, owner, width, cost) in enumerate(mine):
            name = (p, *name)
            index[name] = len(jobs)
            jobs.append((name, owner))
            if name[1] == "ss":
                at = 7
            else:
                held = ("kb", 0, 0) in names[:k + 1] and ("ss",) not in names[:k]
                top = 6 if held else 8
                cursor += cursor % width
                if cursor + width > top:
                    cursor = 0
                at = cursor
                cursor += width
            bank[name] = at
            before[name] = sorted({user[b] for b in range(at, at + width) if b in user}, key=lambda n: index[n])
            for b in range(at, at + width):
                user[b] = name
            counts[owner] += 1
            turn[name] = counts[owner]
            ahead[name] = start + round((end - start) * past / total) if p else 0
            past += cost
        if p:
            done += pass_groups(p - 1)
    return jobs, index, bank, before, turn, ahead


def plan_units(index):
    units, last = [], []

    def add(p, kind, n, *job):
        units.append((p, kind, n))
        last.append(index[(p, *job)])

    for p in range(2 * DEPTH):
        g = p % 2
        nt = len(GROUPS[g])
        for n in range(4):
            add(p, "v", n, "v", nt - 1)
        for n in range(4):
            for kind in "chbu":
                add(p, kind, n, kind, 2 * n + 1)
        for n in range(4):
            for kind in ("ga", "oa", "gb", "ob"):
                add(p, kind, n, kind, 2 * n + 1)
        for n in range(4):
            add(p, "mo", n, "mo", nt - 1)
        if not g:
            for kind in ("k", "vv"):
                for n in range(4):
                    add(p, kind, n, kind, MC - 1)
        for n in range(4):
            add(p, "q", n, "q", 2 * n + 1)
        if g:
            for b in range(NSEQ):
                add(p, "kb", b, "kb", b, MC - 1)
            for b in range(NSEQ):
                add(p, "vb", b, "os", b)
        for n in range(4):
            add(p, "xo", n, "xo", nt - 1)
        for h in range(PH):
            add(p, "pq", h, "pq", 2 * h + 1)
    return units, last


def plan_peer():
    return [(p, i, t, rows) for p in range(2 * DEPTH) for i, (t, rows) in enumerate(GROUPS[p % 2])]


def decoder_step(nc, A, O):
    jobs, JOB, BANK, BEFORE, TURN, AHEAD = plan_jobs()
    peer_tiles = plan_peer()
    peer_groups = [(q, k) for q, tile in enumerate(peer_tiles) for k in range(tile_groups(tile[3]))]
    units, unit_last = plan_units(JOB)
    UNIT = {u: i for i, u in enumerate(units)}
    owner = dict(jobs)

    with ExitStack() as ctx:
        def sb(name, shape, dt=F32):
            return ctx.enter_context(nc.sbuf_tensor(name, shape, dt))

        def sem(name):
            s = ctx.enter_context(nc.semaphore(name))
            sems.append(s)
            return s

        sems = []
        X = sb("X", [P, NTILE, DM])
        NM = GC + NS
        RH = sb("RH", [P, KC * NM])
        RB = sb("RB", [P, 7 * DM])
        RV = sb("RV", [P, 3 * DM])
        W = sb("W", [P, SLOTS * UF])
        T = sb("T", [P, TSLOT, DM])
        acc = sb("acc", [P, DM])
        urow = sb("urow", [P, GRP, DM])
        vrow = sb("vrow", [P, GRP, DM])
        KV = sb("KV", [P, 4 * DM])
        TMP = sb("TMP", [P, 1700])
        ident = sb("ident", [P, P])
        tri = sb("tri", [P, P])
        tri64 = sb("tri64", [NS, NS])
        iota16 = sb("iota16", [P, TOPK])
        iota_i = sb("iota_i", [P, TOPK], I32)
        eps = sb("eps", [P, 1])
        zcarry = sb("zcarry", [P, KC, CW - 1])
        PAR = sb("PAR", [6 * KC, P])
        PARC = sb("PARC", [P, 6 * KC])
        stT = sb("stT", [P, KC, 2 * NSEQ])
        zl = sb("zl", [P, KC, 2 + 2 * NSEQ])
        ssq = sb("ssq", [P, 8])
        std = sb("std", [P, 8])
        rstd = sb("rstd", [P, 8])
        bns = sb("bns", [P, NTILE, 2, 6])
        bna = sb("bna", [P, NTILE, 2])
        rmax = sb("rmax", [P, NTILE, HEADS])
        nmax = sb("nmax", [P, NTILE, HEADS])
        rsum = sb("rsum", [P, NTILE, HEADS])
        rinv = sb("rinv", [P, NTILE, HEADS])
        m16 = sb("m16", [P, 2 * PH, TOPK])
        i16 = sb("i16", [P, 2 * PH, TOPK], U32)
        i16f = sb("i16f", [P, 2 * PH, TOPK])
        tops = sb("tops", [P, PH, TOPK])
        pos = sb("pos", [P, 2, NSEL], U32)
        posf = sb("posf", [P, 2, NSEL])
        sel = sb("sel", [P, 2, NSEL])
        gsum = sb("gsum", [P, PH])
        ginv = sb("ginv", [P, PH])
        gate = sb("gate", [P, TSLOT, NSEL])
        idx = sb("idx", [P, TSLOT, NSEL], U32)
        dots = sb("dots", [P, GRP])
        gel = sb("gel", [P, GRP])
        wts = sb("wts", [P, GRP])
        ps = ctx.enter_context(nc.psum_tensor("ps", [P, 8, 512], F32))

        F = KC * NM
        hT = RH[:, :].rearrange("p (c n) -> p c n", c=KC)
        ssT = RH[:, 2 * DM:2 * DM + 8 * NS]
        state = RH[0:2 * NSEQ, 0:DM]
        sgw8 = RH[0:NS, DM:DM + 64].rearrange("p (g s) -> p g s", g=KC)
        sgw64 = RH[0:NS, DM + 64:DM + 64 + 8 * NS].rearrange("p (g s) -> p g s", g=KC)
        F1 = RB[:, 0:F].rearrange("p (c n) -> p c n", c=KC)
        F2 = RB[:, F:2 * F].rearrange("p (c n) -> p c n", c=KC)
        ln_g = RB[:, 6 * DM:7 * DM]
        mem = RB[:, 0:2 * DM].rearrange("p (m d) -> p m d", m=MC)
        memT = RB[:, 2 * DM:4 * DM].rearrange("p (c n) -> p c n", c=KC)
        ktok = RB[:, 4 * DM:6 * DM].rearrange("p (m d) -> p m d", m=MC)
        qT, oT = F1, F2
        S = RB[:, 0:6 * DM].rearrange("p (t n) -> p t n", t=3)
        XN = RV[:, :].rearrange("p (t d) -> p t d", t=3)
        VT = XN
        mT = RV[:, 0:F].rearrange("p (c n) -> p c n", c=KC)
        PT = RV[:, 0:8 * GC].rearrange("p (i n) -> p i n", i=8)
        probs = [RV[:, 2 * DM:3 * DM], RB[:, 6 * DM:7 * DM]]
        sgT = KV[:, 0:DM].rearrange("p (g t) -> p g t", g=KC)
        sgT64 = KV[0:NS, DM:DM + 8 * NS].rearrange("p (g t) -> p g t", g=KC)
        sg_b = KV[:, 1536:2560].rearrange("p (g t) -> p g t", g=KC)
        ln_b = KV[:, 2560:3584]
        diag = RV[:, 0:2 * GRP * P].rearrange("p (a j n) -> p a j n", a=2, j=GRP)
        kT = KV[:, 0:2 * DM].rearrange("p (c n) -> p c n", c=KC)
        vmem = KV[:, 2 * DM:4 * DM].rearrange("p (m d) -> p m d", m=MC)
        kbT = [kT, RH[:, 0:2 * DM].rearrange("p (c n) -> p c n", c=KC)]
        skeys = KV[:, 0:2 * DM].rearrange("p (i k) -> p i k", i=2 * PH)
        skT = KV[:, 2 * DM:4 * DM].rearrange("p (i n) -> p i n", i=2 * PH)
        NZ = CW - 1 + GC
        z = TMP[:, 0:NZ]
        zs = TMP[:, NZ:NZ + NSEQ * 10].rearrange("p (b n) -> p b n", b=NSEQ)
        tmp = TMP[:, 340:340 + NM]
        cs = [TMP[:, 660:660 + NM], TMP[:, 980:980 + NM]]
        sgw = TMP[:, 0:DM].rearrange("p (g s) -> p g s", g=KC)
        zlo = TMP[0:2 + 2 * NSEQ, 660:660 + DM]
        ptS = TMP[:, 0:8 * NS].rearrange("p (i n) -> p i n", i=8)
        ffn_g = TMP[:, 660:660 + DM]
        qp = [TMP[:, i * 2 * NM:(i + 1) * 2 * NM].rearrange("p (a n) -> p a n", a=2) for i in range(2)]

        def slot(u):
            s = UNIT[u] % SLOTS
            return W[:, s * UF:(s + 1) * UF].rearrange("p (k n) -> p k n", k=KC)

        def cache_slot(u):
            s = UNIT[u] % SLOTS
            return W[:, s * UF:(s + 1) * UF].rearrange("p (m d) -> p m d", m=MC)

        def pf(job):
            return ps[:, BANK[job], 0:ncols(job[0] % 2)]

        def pt(job, rows=P):
            return ps[0:rows, BANK[job]:BANK[job] + 2, :].rearrange("p a n -> p (a n)")

        def chunks(ap):
            return ap.rearrange("p (c n) -> p c n", c=KC)

        job_done = sem("job_done")
        act_evac = sem("act_evac")
        dve_evac = sem("dve_evac")
        unit_in = [sem(f"unit_in{i}") for i in range(SLOTS)]
        act_chain = sem("act_chain")
        dve_chain = sem("dve_chain")
        pool_chain = sem("pool_chain")
        x_in = sem("x_in")
        const_done = sem("const_done")
        par_in = sem("par_in")
        gat_in = sem("gat_in")
        sg8_in = sem("sg8_in")
        sg8_rep = sem("sg8_rep")
        st_in = sem("st_in")
        ln_in = sem("ln_in")
        sgb_in = sem("sgb_in")
        sq_done = sem("sq_done")
        xn_done = sem("xn_done")
        ln_stat = sem("ln_stat")
        ln_std = sem("ln_std")
        vn_done = sem("vn_done")
        zl_done = sem("zl_done")
        zlo_out = sem("zlo_out")
        vn_out = sem("vn_out")
        mem_in = sem("mem_in")
        mem_std = sem("mem_std")
        mem_norm = sem("mem_norm")
        k_out = sem("k_out")
        v_out = sem("v_out")
        kv_in = sem("kv_in")
        max_done = sem("max_done")
        prob_done = sem("prob_done")
        ffn_in = sem("ffn_in")
        skeys_in = sem("skeys_in")
        gexp_in = sem("gexp_in")
        gexp_out = sem("gexp_out")
        idx_done = sem("idx_done")
        u_in = [sem(f"u_in{j}") for j in range(GRP)]
        v_in = [sem(f"v_in{j}") for j in range(GRP)]
        u_read = sem("u_read")
        v_read = sem("v_read")
        diag_done = sem("diag_done")
        merged = sem("merged")
        gel_done = sem("gel_done")
        w_done = sem("w_done")
        x_final = sem("x_final")
        y_done = sem("y_done")
        y_out = sem("y_out")

        class Chain:

            def __init__(self, eng, s):
                self.eng, self.s, self.n = eng, s, 0

            def mark(self, ins):
                self.n += 1
                ins.then_inc(self.s, 1)

            def wait(self):
                self.eng.wait_ge(self.s, self.n)

            def link(self, ins):
                self.mark(ins)
                self.wait()

        def await_job(eng, name):
            eng.wait_ge(job_done, JOB[name] + 1)

        def await_evac(eng, name):
            eng.wait_ge(act_evac if owner[name] == "act" else dve_evac, TURN[name])

        def tiles_to(p, i):
            return sum(len(GROUPS[q % 2]) for q in range(p)) + i + 1

        def norms_to(p, n, i):
            return 3 * tiles_to(p, -1) + n * len(GROUPS[p % 2]) + i + 1

        def layer_of(p):
            return p // 2

        def owned(engine):
            return [n for n, o in jobs if o == engine]

        LAST_SC = [(p, "sc", PH - 1) for p in range(2 * DEPTH)]

        def final_place(t):
            return XN[:, t, :] if t < 3 else RB[:, (t - 3) * DM:(t - 2) * DM] if t < 4 else RB[0:NS, DM:2 * DM]

        def topk_groups(p, i, step):
            first = sum(pass_groups(q) for q in range(p)) + LAG * (i - 1)
            return max(first + round(LAG * min(step, STEPS) / STEPS), 0) if p or i else 0

        stretches = []
        for p in range(2 * DEPTH):
            for i in range(len(GROUPS[p % 2])):
                first, end = topk_groups(p, i, 0), topk_groups(p, i, STEPS)
                if end > first:
                    stretches.append((p, i, first, end))
        psum_acc = ps[:, 0:2, :].rearrange("p a n -> p (a n)")

        block = ctx.enter_context(nc.Block())

        @block.sync
        def _(sp):
            def load_x():
                sp.dma_start(X[:, 0:4, :], A["x_prompt"][0].rearrange("(t p) d -> p t d", p=P)).then_inc(x_in, 16)
                sp.dma_start(X[0:NS, 4, :], A["x_sample"].rearrange("b l d -> (b l) d")).then_inc(x_in, 16)

            def load_vectors(p):
                l = layer_of(p)
                for i, g in enumerate(("g_mix", "g_xattn", "g_mem")):
                    sp.dma_start(PAR[i * KC:(i + 1) * KC, :], A[g][l].rearrange("(c p) -> c p", p=P)).then_inc(par_in, 16)
                sp.dma_start(PAR[3 * KC:6 * KC, :], A["conv_w"][l].rearrange("j (c p) -> (j c) p", p=P)).then_inc(par_in, 16)
                sp.dma_start(sgw, A["sg_w"][l].rearrange("g t s -> t g s")).then_inc(gat_in, 16)
                if p % 2:
                    sp.dma_start(state, A["state_conv"][l].rearrange("b j d -> (b j) d")).then_inc(st_in, 16)
                    for b in range(NSEQ):
                        sp.dma_start(sgw8[b * NDEC:(b + 1) * NDEC, :, :],
                                     A["sg_w"][l, :, 0:NDEC, 0:NDEC].rearrange("g t s -> t g s")).then_inc(sg8_in, 16)
                sp.dma_start(ln_g, A["sg_ln_g"][l].partition_broadcast(P)).then_inc(ln_in, 16)
                sp.dma_start(ln_b, A["sg_ln_b"][l].partition_broadcast(P)).then_inc(ln_in, 16)
                sp.dma_start(sg_b, A["sg_b"][l].partition_broadcast(P)).then_inc(sgb_in, 16)

            def store_values(p):
                l = layer_of(p)
                sp.wait_ge(vn_done, tiles_to(p, 2))
                sp.dma_start(O["new_sg_v_s"][l].rearrange("b l d -> (b l) d"), VT[0:NS, 2, :]).then_inc(vn_out, 16)
                await_evac(sp, (p, "zo"))
                sp.dma_start(O["new_state_conv_p"][l].rearrange("b j d -> (b j) d"), zlo[0:2, :]).then_inc(zlo_out, 16)
                sp.dma_start(O["new_state_conv_s"][l].rearrange("b j d -> (b j) d"),
                             zlo[2:2 + 2 * NSEQ, :]).then_inc(zlo_out, 16)

            def load_memory(p):
                l = layer_of(p)
                await_evac(sp, (p, "ob", KC - 1))
                if p % 2:
                    for m in range(MC):
                        sp.dma_start(ktok[:, m, :], O["new_mem_k_p"][l, 0, m * P:(m + 1) * P].rearrange("p h e -> p (h e)")).then_inc(kv_in, 16)
                        sp.dma_start(vmem[:, m, :], O["new_mem_v_p"][l, 0, m * P:(m + 1) * P].rearrange("p h e -> p (h e)")).then_inc(kv_in, 16)
                else:
                    sp.dma_start(mem, A["mem_prompt"][0].rearrange("(m p) d -> p m d", p=P)).then_inc(mem_in, 16)
                sp.dma_start(ffn_g, A["g_ffn"][l].partition_broadcast(P)).then_inc(ffn_in, 16)

            def store_memory(p, kind, src, name, s):
                l = layer_of(p)
                for m in range(MC):
                    await_evac(sp, (p, kind, m))
                    sp.dma_start(O[name][l, 0, m * P:(m + 1) * P].rearrange("p h e -> p (h e)"), src[:, m, :]).then_inc(s, 16)
                sp.wait_ge(s, 32 * (l + 1))

            def load_subkeys(p):
                sp.dma_start(skeys, A["sub_keys"][layer_of(p)].rearrange("h i n k -> n (h i) k")).then_inc(skeys_in, 16)

            asides = []
            for p in range(2 * DEPTH):
                if p:
                    asides.append((LAST_SC[p - 1], load_vectors, (p,)))
                if p % 2:
                    asides.append(((p, "zo"), store_values, (p,)))
                asides.append(((p, "ob", KC - 1), load_memory, (p,)))
                if not p % 2:
                    asides.append(((p, "k", MC - 1), store_memory, (p, "k", ktok, "new_mem_k_p", k_out)))
                    asides.append(((p, "vv", MC - 1), store_memory, (p, "vv", vmem, "new_mem_v_p", v_out)))
                asides.append(((p, "ss") if p % 2 else (p, "s", 1), load_subkeys, (p,)))
            cols = {"c": ("w_in", 1), "h": ("w_in", 2), "b": ("w_in", 0), "u": ("w_in", 3), "v": ("w_in", 4),
                    "ga": ("w_in", 5), "gb": ("w_in", 6), "oa": ("w_a_out", 0), "ob": ("w_b_out", 0),
                    "mo": ("w_mix_o", 0), "k": ("w_xk", 0), "vv": ("w_xv", 0), "q": ("w_xq", 0),
                    "xo": ("w_xo", 0), "pq": ("w_pq", 0)}
            load_x()
            load_vectors(0)
            for i, (p, kind, n) in enumerate(units):
                if i >= SLOTS:
                    while asides and JOB[asides[0][0]] < unit_last[i - SLOTS]:
                        job, aside, args = asides.pop(0)
                        await_job(sp, job)
                        aside(*args)
                    sp.wait_ge(job_done, unit_last[i - SLOTS] + 1)
                if kind in ("kb", "vb"):
                    src = A["cache_mem_k" if kind == "kb" else "cache_mem_v"][layer_of(p), n]
                    src, dst = src.rearrange("(m p) h e -> p m (h e)", p=P), cache_slot((p, kind, n))
                else:
                    name, part = cols[kind]
                    c0 = part * DM + n * UW
                    src = A[name][layer_of(p), :, c0:c0 + UW].rearrange("(k p) n -> p k n", p=P)
                    dst = slot((p, kind, n))
                sp.dma_start(dst, src).then_inc(unit_in[i % SLOTS], 16)
            assert not asides
            await_job(sp, LAST_SC[-1])
            sp.dma_start(ffn_g, A["g_final"].partition_broadcast(P)).then_inc(ffn_in, 16)
            for t in range(NTILE):
                sp.wait_ge(y_done, t + 1)
                dst = O["y_prompt"][0, t * P:(t + 1) * P, :] if t < 4 else O["y_sample"].rearrange("b l d -> (b l) d")
                src = final_place(t)
                sp.dma_start(dst, src).then_inc(y_out, 16)
            for s, n in ((vn_out, DEPTH), (zlo_out, 2 * DEPTH), (k_out, 2 * DEPTH), (v_out, 2 * DEPTH), (y_out, NTILE)):
                sp.wait_ge(s, 16 * n)

        @block.gpsimd
        def _(pool):
            ch = Chain(pool, pool_chain)
            ch.mark(pool.memset(ident[:, :], 0.0))
            ch.mark(pool.memset(tri[:, :], 1.0))
            ch.mark(pool.memset(tri64[:, :], 1.0))
            ch.mark(pool.iota(iota_i[:, :], pattern=[[1, TOPK]], base=0, channel_multiplier=0))
            ch.wait()
            ch.mark(pool.affine_select(out=ident[:, :], in_=ident[:, :], compare_op=ALU.not_equal, fill=1.0,
                                       base=0, pattern=[[-1, P]], channel_multiplier=1))
            ch.mark(pool.affine_select(out=tri[:, :], in_=tri[:, :], compare_op=ALU.is_ge, fill=0.0,
                                       base=0, pattern=[[1, P]], channel_multiplier=-1))
            ch.mark(pool.tensor_copy(iota16[:, :], iota_i[:, :]))
            t64 = tri64[:, :].rearrange("p (b t) -> p b t", b=NSEQ)
            ch.link(pool.affine_select(out=t64, in_=t64, compare_op=ALU.is_ge, fill=0.0,
                                       base=0, pattern=[[8, 8], [1, 8]], channel_multiplier=-1))
            pool.affine_select(out=t64, in_=t64, compare_op=ALU.is_ge, fill=0.0,
                               base=0, pattern=[[-8, 8], [0, 8]], channel_multiplier=1).then_inc(const_done, 1)
            tables = [A[name].rearrange("l n d -> (l n) d") for name in ("peer_u", "peer_v")]
            n = 0
            for q, (p, i, t, rows) in enumerate(peer_tiles):
                pool.wait_ge(idx_done, q + 1)
                for k in range(tile_groups(rows)):
                    for table, ring, read, landed in zip(tables, (urow, vrow), (u_read, v_read), (u_in, v_in)):
                        for j in range(GRP):
                            if n:
                                pool.wait_ge(read, (n - 1) * GRP + j + 1)
                            e = k * GRP + j
                            pool.indirect_dma_start(
                                ring[:, j, :], None, table,
                                bass.IndirectOffsetOnAxis(ap=idx[:, q % TSLOT, e:e + 1], axis=0)).then_inc(landed[j], 16)
                    n += 1

        @block.tensor
        def _(pe):
            started = []

            def begin(name):
                assert jobs[len(started)][0] == name, (jobs[len(started)], name)
                started.append(name)
                for b in BEFORE[name]:
                    await_evac(pe, b)

            def end(ins):
                ins.then_inc(job_done, 1)

            def await_unit(u):
                i = UNIT[u]
                pe.wait_ge(unit_in[i % SLOTS], 16 * (i // SLOTS + 1))

            def transposes(name, ins, rows_in, cols, step=P):
                begin(name)
                for i, a in enumerate(ins):
                    m = pe.transpose(ps[0:cols, BANK[name] + i * step // 512, i * step % 512:i * step % 512 + rows_in],
                                     a, ident[0:rows_in, 0:rows_in])
                end(m)

            def project(name, c, src):
                u = (name[0], name[1], c // 2)
                begin(name)
                if c % 2 == 0:
                    await_unit(u)
                for k in range(KC):
                    m = pe.matmul(pf(name), slot(u)[:, k, (c % 2) * P:(c % 2) * P + P], src[:, k, 0:ncols(name[0] % 2)],
                                  start=(k == 0), stop=(k == KC - 1))
                end(m)

            def project_tokens(name, src, i, rows):
                begin(name)
                for a in range(2):
                    for b in range(2):
                        u = (name[0], name[1], 2 * a + b)
                        if i == 0:
                            await_unit(u)
                        for k in range(KC):
                            m = pe.matmul(ps[0:rows, BANK[name] + a, b * UW:(b + 1) * UW],
                                          src[:, k, i * P:i * P + rows], slot(u)[:, k, :],
                                          start=(k == 0), stop=(k == KC - 1))
                end(m)

            def trunk(p):
                l, g = layer_of(p), p % 2
                tiles = GROUPS[g]
                nt = len(tiles)

                def norm_transposes(n):
                    for i, (t, rows) in enumerate(tiles):
                        pe.wait_ge(xn_done, norms_to(p, n, i))
                        src = XN[:, i, :] if n < 2 else T[:, (tiles_to(p, i) - 1) % TSLOT, :]
                        transposes((p, "n", n, i), [src[0:rows, c * P:(c + 1) * P] for c in range(KC)], rows, P)
                    await_evac(pe, (p, "n", n, nt - 1))

                pe.wait_ge(par_in, 64 * (p + 1))
                transposes((p, "par"), [PAR[:, :]], 6 * KC, P)
                if g:
                    pe.wait_ge(st_in, 16 * (l + 1))
                    transposes((p, "st"), [state[:, c * P:(c + 1) * P] for c in range(KC)], 2 * NSEQ, P, 2 * NSEQ)
                pe.wait_ge(gat_in, 16 * (p + 1))
                transposes((p, "sw"), [sgw[:, c, :] for c in range(KC)], P, P)
                if g:
                    pe.wait_ge(sg8_rep, l + 1)
                    transposes((p, "sw64"), [sgw64[:, c, :] for c in range(KC)], NS, NS, NS)
                norm_transposes(0)
                for i, (t, rows) in enumerate(tiles):
                    project_tokens((p, "v", i), hT, i, rows)
                for c in range(KC):
                    for kind in "chbu":
                        project((p, kind, c), c, hT)
                if g:
                    pe.wait_ge(zl_done, KC * (l + 1))
                    transposes((p, "zo"), [zl[:, c, :] for c in range(KC)], P, 2 + 2 * NSEQ)
                pe.wait_ge(vn_done, tiles_to(p, nt - 1))
                for c in range(KC):
                    begin((p, "mx", c))
                    out = pf((p, "mx", c))
                    for i in range(2):
                        m = pe.matmul(out[:, i * P:(i + 1) * P], VT[:, i, c * P:(c + 1) * P], sgT[:, c, :], start=True, stop=True)
                    if g:
                        m = pe.matmul(out[:, GC:GC + NS], VT[0:NS, 2, c * P:(c + 1) * P], sgT64[:, c, :], start=True, stop=True)
                    end(m)
                await_evac(pe, (p, "mx", KC - 1))
                for c in range(KC):
                    project((p, "ga", c), c, hT)
                    project((p, "oa", c), c, F1)
                    project((p, "gb", c), c, hT)
                    project((p, "ob", c), c, F2)
                await_evac(pe, (p, "ob", KC - 1))
                for i, (t, rows) in enumerate(tiles):
                    project_tokens((p, "mo", i), mT, i, rows)
                if g:
                    pe.wait_ge(kv_in, 64 * (l + 1))
                else:
                    pe.wait_ge(mem_norm, l + 1)
                    for m in range(MC):
                        transposes((p, "mt", m), [mem[:, m, c * P:(c + 1) * P] for c in range(KC)], P, P)
                    await_evac(pe, (p, "mt", MC - 1))
                    for kind in ("k", "vv"):
                        for m in range(MC):
                            project_tokens((p, kind, m), memT, m, P)
                    await_evac(pe, (p, "k", MC - 1))
                for m in range(MC):
                    transposes((p, "kt", m), [ktok[:, m, c * P:(c + 1) * P] for c in range(KC)], P, P)
                norm_transposes(1)
                for c in range(KC):
                    project((p, "q", c), c, hT)
                await_evac(pe, (p, "q", KC - 1))

                def prompt_scores(i):
                    begin((p, "s", i))
                    out = pt((p, "s", i))
                    for h in range(HEADS):
                        for e in range(2):
                            m = pe.matmul(out[:, h * NMEM:(h + 1) * NMEM], qT[:, 2 * h + e, i * P:(i + 1) * P],
                                          kT[:, 2 * h + e, :], start=(e == 0), stop=(e == 1))
                    end(m)

                def prob_transposes(i, rows):
                    pe.wait_ge(prob_done, tiles_to(p, i))
                    transposes((p, "pt", i), [probs[i % 2][0:rows, j * P:(j + 1) * P] for j in range(8)], rows, P)

                def key_transposes(b):
                    await_unit((p, "kb", b))
                    for m in range(MC):
                        transposes((p, "kb", b, m), [cache_slot((p, "kb", b))[:, m, c * P:(c + 1) * P] for c in range(KC)], P, P)

                def sample_scores(b):
                    for m in range(MC):
                        await_evac(pe, (p, "kb", b, m))
                    for h in range(HEADS):
                        for m in range(MC):
                            col = (2 * h + m) * NS + b * NDEC
                            for e in range(2):
                                last = pe.matmul(ps[:, BANK[p, "ss"], col:col + NDEC],
                                                 kbT[b % 2][:, 2 * h + e, m * P:(m + 1) * P],
                                                 qT[:, 2 * h + e, GC + b * NDEC:GC + (b + 1) * NDEC],
                                                 start=(e == 0), stop=(e == 1))
                    return last

                prompt_scores(0)
                prompt_scores(1)
                prob_transposes(0, P)
                if g:
                    key_transposes(0)
                prob_transposes(1, P)
                if g:
                    for b in BEFORE[p, "ss"]:
                        await_evac(pe, b)
                    for b in range(1, NSEQ):
                        key_transposes(b)
                        sample_scores(b - 1)
                    last = sample_scores(NSEQ - 1)
                    started.append((p, "ss"))
                    end(last)
                    await_evac(pe, (p, "ss"))
                    transposes((p, "sb"), [ssT[:, j * NS:(j + 1) * NS] for j in range(8)], P, NS)
                await_evac(pe, (p, "pt", 1))
                for c in range(KC):
                    begin((p, "o", c))
                    for m in range(MC):
                        last = pe.matmul(ps[:, BANK[p, "o", c], 0:GC], vmem[:, m, c * P:(c + 1) * P],
                                         PT[:, (c // 2) * 2 + m, :], start=(m == 0), stop=(m == MC - 1))
                    end(last)
                if g:
                    prob_transposes(2, NS)
                    await_evac(pe, (p, "pt", 2))
                    for b in range(NSEQ):
                        await_unit((p, "vb", b))
                        begin((p, "os", b))
                        for c in range(KC):
                            for m in range(MC):
                                last = pe.matmul(ps[:, BANK[p, "os", b], c * NDEC:(c + 1) * NDEC],
                                                 cache_slot((p, "vb", b))[:, m, c * P:(c + 1) * P],
                                                 ptS[:, (c // 2) * 2 + m, b * NDEC:(b + 1) * NDEC],
                                                 start=(m == 0), stop=(m == MC - 1))
                        end(last)
                    await_evac(pe, (p, "os", NSEQ - 1))
                await_evac(pe, (p, "o", KC - 1))
                for i, (t, rows) in enumerate(tiles):
                    project_tokens((p, "xo", i), oT, i, rows)
                pe.wait_ge(skeys_in, 16 * (p + 1))
                for i in range(2):
                    transposes((p, "sk", i), [skeys[:, 8 * i + j, :] for j in range(8)], P, P)
                norm_transposes(2)
                for c in range(2):
                    project((p, "pq", c), c, hT)
                for h in range(PH):
                    if h + 1 < PH:
                        for c in (2 * h + 2, 2 * h + 3):
                            project((p, "pq", c), c, hT)
                    begin((p, "sc", h))
                    await_evac(pe, (p, "pq", 2 * h + 1))
                    for i, (t, rows) in enumerate(tiles):
                        for j in range(2):
                            col = i * 256 + j * P
                            m = pe.matmul(ps[0:rows, BANK[p, "sc", h] + col // 512, col % 512:col % 512 + P],
                                          qp[h % 2][:, j, i * P:i * P + rows], skT[:, 2 * h + j, :], start=True, stop=True)
                    end(m)

            def peer_products(k, first, after):
                if k:
                    pe.wait_ge(merged, k)
                for n in range(first, after):
                    pe.wait_ge(diag_done, sum(b - a for _, _, a, b in stretches[:k]) + n - first + 1)
                    for j in range(GRP):
                        pe.wait_ge(v_in[j], 16 * (n + 1))
                        for b in range(2):
                            m = pe.matmul(ps[:, b, :], diag[:, n % 2, j, :], vrow[:, j, b * 512:(b + 1) * 512],
                                          start=(n == first and j == 0), stop=(n == after - 1 and j == GRP - 1))
                        m.then_inc(v_read, 1)

            pe.wait_ge(const_done, 1)
            for p in range(2 * DEPTH):
                trunk(p)
                await_evac(pe, LAST_SC[p])
                for k, stretch in enumerate(stretches):
                    if stretch[0] == p:
                        peer_products(k, *stretch[2:])
                pe.wait_ge(merged, sum(at <= p for at, _, _, _ in stretches))
            assert len(started) == len(jobs)

        @block.scalar
        def _(act):
            ch = Chain(act, act_chain)
            mine, seen, groups = owned("act"), [], [0]

            def peer_to(n):
                while groups[0] < n:
                    act.wait_ge(u_read, (groups[0] + 1) * GRP)
                    act.activation(gel[:, :], dots[:, :], ACT.Gelu_apprx_tanh).then_inc(gel_done, 1)
                    groups[0] += 1

            def finished(name):
                peer_to(AHEAD[name])
                await_job(act, name)

            def emptied(name):
                peer_to(AHEAD[name])
                await_evac(act, name)

            def take(name):
                assert mine[len(seen)] == name, (mine[len(seen)], name)
                seen.append(name)
                finished(name)

            def evac(name, out, in_, func=ACT.Copy):
                take(name)
                act.activation(out, in_, func).then_inc(act_evac, 1)

            def gate_exps(p):
                for i, (t, rows) in enumerate(GROUPS[p % 2]):
                    q = tiles_to(p, i) - 1
                    peer_to(topk_groups(p, i, GATE_STEP))
                    act.wait_ge(gexp_in, q + 1)
                    act.activation(tops[0:rows, :, :], tops[0:rows, :, :], ACT.Exp).then_inc(gexp_out, 1)
                    peer_to(topk_groups(p, i, STEPS))

            def trunk(p):
                l, g = layer_of(p), p % 2
                tiles = GROUPS[g]
                nt = len(tiles)

                def squares(n):
                    for i, (t, rows) in enumerate(tiles):
                        if n == 0 and l:
                            act.wait_ge(x_final, tiles_to(p - 2, i))
                        if n == 1:
                            finished((p, "mo", nt - 1))
                        if n == 2:
                            finished((p, "o", KC - 1))
                        if n:
                            emptied((p, "mo" if n == 1 else "xo", i))
                        ch.mark(act.activation(XN[0:rows, i, :], X[0:rows, t, :], ACT.Square, accum_out=ssq[0:rows, i:i + 1]))
                    ch.wait()
                    act.activation(std[:, 0:nt], ssq[:, 0:nt], ACT.Sqrt, bias=eps[:, :], scale=1.0 / DM).then_inc(sq_done, 1)

                evac((p, "par"), PARC[:, :], ps[:, BANK[p, "par"], 0:6 * KC])
                if g:
                    evac((p, "st"), stT[:, :, :], chunks(ps[:, BANK[p, "st"], 0:KC * 2 * NSEQ]))
                squares(0)
                for i, (t, rows) in enumerate(tiles):
                    take((p, "v", i))
                    finished((p, "n", 0, nt - 1))
                    act.activation(VT[0:rows, i, :], pt((p, "v", i), rows), ACT.Gelu_apprx_tanh).then_inc(act_evac, 1)
                act.wait_ge(ln_stat, tiles_to(p, nt - 1))
                act.activation(std[:, 0:nt], bna[:, 0:nt, 1], ACT.Sqrt, bias=eps[:, :]).then_inc(ln_std, 1)
                n = ncols(g)
                for c in range(KC):
                    if c >= 2:
                        emptied((p, "h", c - 2))
                    evac((p, "c", c), cs[c % 2][:, 0:n], pf((p, "c", c)))
                    evac((p, "u", c), F2[:, c, 0:n], pf((p, "u", c)), ACT.Gelu_apprx_tanh)
                if g:
                    emptied((p, "h", KC - 1))
                    evac((p, "zo"), zlo, pt((p, "zo"), 2 + 2 * NSEQ))
                    act.wait_ge(zlo_out, 32 * (l + 1))
                for c in range(KC):
                    emptied((p, "oa", c - 1) if c else (p, "h", KC - 1))
                    evac((p, "ga", c), cs[0][:, 0:n], pf((p, "ga", c)), ACT.Sigmoid)
                    if c:
                        emptied((p, "ob", c - 1))
                    evac((p, "gb", c), cs[1][:, 0:n], pf((p, "gb", c)), ACT.Sigmoid)
                if not g:
                    emptied((p, "ob", KC - 1))
                    act.wait_ge(mem_in, 16 * (l + 1))
                    for m in range(MC):
                        ch.mark(act.activation(RB[:, (2 + m) * DM:(3 + m) * DM], mem[:, m, :], ACT.Square,
                                               accum_out=ssq[:, 5 + m:6 + m]))
                    ch.wait()
                    act.activation(std[:, 5:7], ssq[:, 5:7], ACT.Sqrt, bias=eps[:, :], scale=1.0 / DM).then_inc(mem_std, 1)
                squares(1)
                if not g:
                    for m in range(MC):
                        evac((p, "k", m), ktok[:, m, :], pt((p, "k", m)))
                    for m in range(MC):
                        evac((p, "vv", m), vmem[:, m, :], pt((p, "vv", m)))
                for c in range(KC):
                    evac((p, "q", c), qT[:, c, 0:n], pf((p, "q", c)))

                def exps(i, rows, name):
                    take(name)
                    act.wait_ge(max_done, tiles_to(p, i))
                    if i >= 2:
                        finished((p, "pt", i - 2))
                    for h in range(HEADS):
                        e = act.activation(probs[i % 2][0:rows, h * NMEM:(h + 1) * NMEM],
                                           pt(name, rows)[:, h * NMEM:(h + 1) * NMEM], ACT.Exp,
                                           bias=nmax[0:rows, i, h:h + 1], scale=1.0 / 16.0,
                                           accum_out=rsum[0:rows, i, h:h + 1])
                    e.then_inc(act_evac, 1)

                def evac_probs(i):
                    evac((p, "pt", i), PT[:, :, i * P:(i + 1) * P], chunks(pt((p, "pt", i))))

                def evac_keys(b):
                    evac((p, "kb", b, 0), kbT[b % 2][:, :, 0:P], chunks(pt((p, "kb", b, 0))))

                exps(0, P, (p, "s", 0))
                exps(1, P, (p, "s", 1))
                evac_probs(0)
                if g:
                    evac_keys(0)
                evac_probs(1)
                if g:
                    for b in range(1, NSEQ):
                        evac_keys(b)
                    evac((p, "ss"), ssT, ps[:, BANK[p, "ss"], :])
                    exps(2, NS, (p, "sb"))
                if not g:
                    act.wait_ge(k_out, 32 * (l + 1))
                for c in range(KC):
                    evac((p, "o", c), oT[:, c, 0:GC], ps[:, BANK[p, "o", c], 0:GC])
                if g:
                    evac((p, "pt", 2), ptS, chunks(pt((p, "pt", 2)))[:, :, 0:NS])
                squares(2)
                for h in range(PH):
                    for c in range(0 if h == 0 else 2 * h + 2, min(2 * h + 4, 2 * PH)):
                        evac((p, "pq", c), qp[c // 2 % 2][:, c % 2, 0:n], pf((p, "pq", c)))
                    name = (p, "sc", h)
                    take(name)
                    e = act.activation(S[:, 0:2, h * 256:(h + 1) * 256],
                                       ps[:, BANK[name], :].rearrange("p (t n) -> p t n", t=2), ACT.Copy)
                    if g:
                        e = act.activation(S[0:NS, 2, h * 256:(h + 1) * 256], ps[0:NS, BANK[name] + 1, 0:256], ACT.Copy)
                    e.then_inc(act_evac, 1)

            for p in range(2 * DEPTH):
                if p:
                    gate_exps(p - 1)
                    act.wait_ge(idx_done, tiles_to(p - 1, len(GROUPS[(p - 1) % 2]) - 1))
                    act.wait_ge(merged, sum(at < p for at, _, _, _ in stretches))
                else:
                    act.wait_ge(const_done, 2)
                    act.wait_ge(x_in, 32)
                trunk(p)
            assert len(seen) == len(mine)
            gate_exps(2 * DEPTH - 1)
            peer_to(len(peer_groups))
            act.wait_ge(x_final, len(peer_tiles))
            for t in range(NTILE):
                rows = NS if t == 4 else P
                ch.mark(act.activation(final_place(t), X[0:rows, t, :], ACT.Square, accum_out=ssq[0:rows, t:t + 1]))
            ch.wait()
            act.activation(std[:, 0:NTILE], ssq[:, 0:NTILE], ACT.Sqrt, bias=eps[:, :], scale=1.0 / DM).then_inc(sq_done, 1)

        @block.vector
        def _(dve):
            ch = Chain(dve, dve_chain)
            mine, seen, groups = owned("dve"), [], [0]

            def finish(q):
                t, rows = peer_tiles[q][2:]
                x, a = X[0:rows, t, :], acc[0:rows, :]
                if rows < P:
                    ch.link(dve.tensor_tensor(x, x, a, ALU.add))
                    ch.link(dve.tensor_copy(a, acc[rows:P, :]))
                dve.tensor_tensor(x, x, a, ALU.add).then_inc(x_final, 1)
                dve.wait_ge(x_final, q + 1)

            def merge(k):
                first, end = stretches[k][2:]
                dve.wait_ge(v_read, end * GRP)
                if peer_groups[first][1] == 0:
                    ins = dve.tensor_copy(acc[:, :], psum_acc)
                else:
                    ins = dve.tensor_tensor(acc[:, :], acc[:, :], psum_acc, ALU.add)
                ins.then_inc(merged, 1)
                dve.wait_ge(merged, k + 1)
                q, last = peer_groups[end - 1]
                if last == tile_groups(peer_tiles[q][3]) - 1:
                    finish(q)

            def peer_group():
                n = groups[0]
                q, k = peer_groups[n]
                t, rows = peer_tiles[q][2:]
                r, kept = slice(0, P), q % TSLOT
                for j in range(GRP):
                    dve.wait_ge(u_in[j], 16 * (n + 1))
                    dve.tensor_tensor_reduce(urow[r, j, :], urow[r, j, :], T[r, kept, :], 1.0, 0.0, ALU.mult, ALU.add,
                                             dots[r, j:j + 1]).then_inc(u_read, 1)
                dve.wait_ge(gel_done, n + 1)
                dve.tensor_tensor(wts[r, :], gel[r, :], gate[r, kept, k * GRP:(k + 1) * GRP], ALU.mult).then_inc(w_done, 1)
                dve.wait_ge(w_done, n + 1)
                groups[0] += 1
                if any(first <= n < end for _, _, first, end in stretches):
                    starts = any(first == n for _, _, first, end in stretches)
                    if n:
                        dve.wait_ge(v_read, (n if starts else n - 1) * GRP)
                    dve.tensor_tensor(diag[:, n % 2, :, :], ident[:, :].unsqueeze(1).to_broadcast([P, GRP, P]),
                                      wts[:, :].unsqueeze(2).to_broadcast([P, GRP, P]), ALU.mult).then_inc(diag_done, 1)
                    return
                for j in range(GRP):
                    dve.wait_ge(v_in[j], 16 * (n + 1))
                    if n or j:
                        dve.wait_ge(v_read, n * GRP + j)
                    if k == 0 and j == 0:
                        ins = dve.tensor_scalar(acc[r, :], vrow[r, j, :], wts[r, j:j + 1], None, ALU.mult)
                    else:
                        ins = dve.scalar_tensor_tensor(out=acc[r, :], in0=vrow[r, j, :], scalar=wts[r, j:j + 1],
                                                       in1=acc[r, :], op0=ALU.mult, op1=ALU.add)
                    ins.then_inc(v_read, 1)
                if k == tile_groups(rows) - 1:
                    dve.wait_ge(v_read, (n + 1) * GRP)
                    finish(q)

            def peer_to(n):
                while groups[0] < n:
                    peer_group()

            def emptied(name):
                peer_to(AHEAD[name])
                await_evac(dve, name)

            def take(name):
                assert mine[len(seen)] == name, (mine[len(seen)], name)
                seen.append(name)
                peer_to(AHEAD[name])
                await_job(dve, name)

            def done(ins):
                ins.then_inc(dve_evac, 1)

            def top_k(p, i):
                t, rows = GROUPS[p % 2][i]
                q = tiles_to(p, i) - 1
                r, kept = slice(0, rows), q % TSLOT
                step = [0]

                def breathe():
                    step[0] += 1
                    peer_to(topk_groups(p, i, step[0]))

                Si = S[r, i, :]
                part = [Si[:, j * P:(j + 1) * P] for j in range(2 * PH)]
                cand = [Si[:, h * 256:(h + 1) * 256] for h in range(PH)]

                def top16(src, vals, where):
                    def each(op):
                        for first in range(0, len(src), 8):
                            for n in range(first, first + 8):
                                ch.mark(op(where[n], vals[n], src[n]))
                            breathe()
                        ch.wait()
                    each(lambda w, v, s: dve.max(v[:, 0:8], s))
                    each(lambda w, v, s: dve.max_index(w[:, 0:8], v[:, 0:8], s))
                    each(lambda w, v, s: dve.match_replace(s, v[:, 0:8], s, LOWEST))
                    each(lambda w, v, s: dve.max(v[:, 8:16], s))
                    each(lambda w, v, s: dve.max_index(w[:, 8:16], v[:, 8:16], s))

                if rows < P:
                    dve.wait_ge(xn_done, norms_to(p, 2, i))
                    ch.mark(dve.tensor_copy(T[rows:P, kept, :], T[r, kept, :]))
                top16(part, [m16[r, j, :] for j in range(2 * PH)], [i16[r, j, :] for j in range(2 * PH)])
                ch.mark(dve.tensor_copy(i16f[r, :, :], i16[r, :, :]))
                mm = m16[r, :, :].rearrange("p (h i) n -> p h i n", i=2)
                ch.link(dve.tensor_tensor(Si.rearrange("p (h a b) -> p h a b", h=PH, a=TOPK),
                                          mm[:, :, 0, :].unsqueeze(3).to_broadcast([rows, PH, TOPK, TOPK]),
                                          mm[:, :, 1, :].unsqueeze(2).to_broadcast([rows, PH, TOPK, TOPK]), ALU.add))
                top16(cand, [tops[r, h, :] for h in range(PH)], [pos[r, 0, h * TOPK:(h + 1) * TOPK] for h in range(PH)])
                assert step[0] == GATE_STEP
                gt = gate[r, kept, :].rearrange("p (h n) -> p h n", h=PH)
                ch.link(dve.tensor_tensor(gt, tops[r, :, :], tops[r, :, 0:1].to_broadcast([rows, PH, TOPK]), ALU.subtract))
                dve.tensor_copy(tops[r, :, :], gt).then_inc(gexp_in, 1)
                ch.link(dve.tensor_single_scalar(pos[r, 1, :], pos[r, 0, :], 15, ALU.bitwise_and))
                ch.link(dve.tensor_single_scalar(pos[r, 0, :], pos[r, 0, :], 4, ALU.logical_shift_right))
                ch.link(dve.tensor_copy(posf[r, :, :], pos[r, :, :]))
                ii = i16f[r, :, :].rearrange("p (h i) n -> p h i n", i=2)
                oh = Si.rearrange("p (s j) -> p s j", j=TOPK)
                oh4 = Si.rearrange("p (h s j) -> p h s j", h=PH, j=TOPK)
                for j in range(2):
                    ch.link(dve.tensor_tensor(oh, posf[r, j, :].unsqueeze(2).to_broadcast([rows, NSEL, TOPK]),
                                              iota16[r, :].unsqueeze(1).to_broadcast([rows, NSEL, TOPK]), ALU.is_equal))
                    ch.link(dve.tensor_tensor(oh4, oh4, ii[:, :, j, :].unsqueeze(2).to_broadcast([rows, PH, TOPK, TOPK]), ALU.mult))
                    breathe()
                    ch.link(dve.tensor_reduce(sel[r, j, :], oh, AX, ALU.add))
                    breathe()
                ch.link(dve.scalar_tensor_tensor(out=sel[r, 0, :], in0=sel[r, 0, :], scalar=float(NK), in1=sel[r, 1, :],
                                                 op0=ALU.mult, op1=ALU.add))
                ins = dve.tensor_scalar(idx[r, kept, :], sel[r, 0, :], float(NE * layer_of(p)), None, ALU.add)
                half = NSEL * rows // P
                if rows < P:
                    ch.link(ins)
                    ins = dve.tensor_copy(idx[rows:P, kept, 0:half], idx[r, kept, half:NSEL])
                ins.then_inc(idx_done, 1)
                dve.wait_ge(gexp_out, q + 1)
                ch.link(dve.tensor_reduce(gsum[r, :], tops[r, :, :], AX, ALU.add))
                ch.link(dve.reciprocal(ginv[r, :], gsum[r, :]))
                ch.link(dve.tensor_tensor(gt, tops[r, :, :], ginv[r, :].unsqueeze(2).to_broadcast([rows, PH, TOPK]), ALU.mult))
                if rows < P:
                    ch.link(dve.tensor_copy(gate[rows:P, kept, 0:half], gate[r, kept, half:NSEL]))
                for k, stretch in enumerate(stretches):
                    if stretch[0:2] == (p, i):
                        merge(k)

            def trunk(p):
                l, g = layer_of(p), p % 2
                tiles = GROUPS[g]
                nt = len(tiles)
                n = ncols(g)

                def gain(i):
                    return PARC[:, i * KC:(i + 1) * KC]

                def norm(k):
                    dve.wait_ge(sq_done, 3 * p + k + 1)
                    ch.link(dve.reciprocal(rstd[:, 0:nt], std[:, 0:nt]))
                    if k == 2:
                        dve.wait_ge(ffn_in, 16 * (p + 1))
                    for i, (t, rows) in enumerate(tiles):
                        if k == 2:
                            ins = dve.scalar_tensor_tensor(out=T[0:rows, (tiles_to(p, i) - 1) % TSLOT, :], in0=X[0:rows, t, :],
                                                           scalar=rstd[0:rows, i:i + 1], in1=ffn_g[0:rows, :],
                                                           op0=ALU.mult, op1=ALU.mult)
                        else:
                            ins = dve.tensor_scalar(XN[0:rows, i, :], X[0:rows, t, :], rstd[0:rows, i:i + 1], None, ALU.mult)
                        ins.then_inc(xn_done, 1)
                    for i, (t, rows) in enumerate(tiles):
                        take((p, "n", k, i))
                        src = chunks(pt((p, "n", k, i)))[:, :, 0:rows]
                        dst = hT[:, :, i * P:i * P + rows]
                        if k == 2:
                            done(dve.tensor_copy(dst, src))
                        else:
                            done(dve.tensor_tensor(dst, src, gain(k).unsqueeze(2).to_broadcast([P, KC, rows]), ALU.mult))

                if g:
                    dve.wait_ge(sg8_in, 16 * NSEQ * (l + 1))
                    s64 = sgw64.rearrange("p g (b s) -> p g b s", b=NSEQ)
                    for c in range(KC):
                        rep = dve.tensor_copy(s64[:, c], sgw8[:, c, :].unsqueeze(1).to_broadcast([NS, NSEQ, NDEC]))
                    rep.then_inc(sg8_rep, 1)
                take((p, "sw"))
                done(dve.tensor_tensor(sgT, chunks(pt((p, "sw"))), tri[:, :].unsqueeze(1).to_broadcast([P, KC, P]), ALU.mult))
                if g:
                    take((p, "sw64"))
                    done(dve.tensor_tensor(sgT64, chunks(ps[0:NS, BANK[p, "sw64"], :]),
                                           tri64[:, :].unsqueeze(1).to_broadcast([NS, KC, NS]), ALU.mult))
                emptied((p, "par"))
                norm(0)
                for i, (t, rows) in enumerate(tiles):
                    emptied((p, "v", i))
                    for j in range(2):
                        ch.mark(dve.bn_stats(bns[0:rows, i, j, :], VT[0:rows, i, j * 512:(j + 1) * 512]))
                    ch.wait()
                    dve.bn_aggr(bna[0:rows, i, :], bns[0:rows, i, :, :]).then_inc(ln_stat, 1)
                dve.wait_ge(ln_std, p + 1)
                ch.link(dve.reciprocal(rstd[:, 0:nt], std[:, 0:nt]))
                dve.wait_ge(ln_in, 32 * (p + 1))
                for i, (t, rows) in enumerate(tiles):
                    v = VT[0:rows, i, :]
                    ch.link(dve.tensor_scalar(v, v, bna[0:rows, i, 0:1], rstd[0:rows, i:i + 1], ALU.subtract, ALU.mult))
                    ch.link(dve.tensor_tensor(v, v, ln_g[0:rows, :], ALU.mult))
                    dve.tensor_tensor(v, v, ln_b[0:rows, :], ALU.add).then_inc(vn_done, 1)
                if not g:
                    ch.mark(dve.memset(z[:, 0:CW - 1], 0.0))
                ts = tmp[:, GC:NM].rearrange("p (b n) -> p b n", b=NSEQ)
                for c in range(KC):
                    def tap(j):
                        i = 3 * KC + j * KC + c
                        return PARC[:, i:i + 1]
                    emptied((p, "c", c))
                    take((p, "h", c))
                    hp, src = pf((p, "h", c)), cs[c % 2]
                    ins = dve.tensor_tensor(z[:, 2:NZ], hp[:, 0:GC], src[:, 0:GC], ALU.mult)
                    if g:
                        ch.mark(ins)
                        ch.mark(dve.tensor_copy(z[:, 0:2], zcarry[:, c, :]))
                        ch.mark(dve.tensor_copy(zs[:, :, 0:2], stT[:, c, :].rearrange("p (b j) -> p b j", b=NSEQ)))
                        ins = dve.tensor_tensor(zs[:, :, 2:10], hp[:, GC:NM].rearrange("p (b n) -> p b n", b=NSEQ),
                                                src[:, GC:NM].rearrange("p (b n) -> p b n", b=NSEQ), ALU.mult)
                    done(ins)
                    ch.wait()
                    emptied((p, "h", c))
                    if g:
                        ch.mark(dve.tensor_copy(zl[:, c, 0:2], z[:, GC:NZ]))
                        dve.tensor_copy(zl[:, c, 2:2 + 2 * NSEQ].rearrange("p (b j) -> p b j", b=NSEQ),
                                        zs[:, :, 8:10]).then_inc(zl_done, 1)
                        ch.mark(dve.tensor_scalar(ts, zs[:, :, 0:8], tap(0), None, ALU.mult))
                    else:
                        ch.mark(dve.tensor_copy(zcarry[:, c, :], z[:, GC:NZ]))
                    ch.mark(dve.tensor_scalar(tmp[:, 0:GC], z[:, 0:GC], tap(0), None, ALU.mult))
                    for j in (1, 2):
                        ch.wait()
                        ch.mark(dve.scalar_tensor_tensor(out=tmp[:, 0:GC], in0=z[:, j:j + GC], scalar=tap(j),
                                                         in1=tmp[:, 0:GC], op0=ALU.mult, op1=ALU.add))
                        if g:
                            ch.mark(dve.scalar_tensor_tensor(out=ts, in0=zs[:, :, j:j + 8], scalar=tap(j),
                                                             in1=ts, op0=ALU.mult, op1=ALU.add))
                    ch.wait()
                    if g:
                        dve.wait_ge(zl_done, KC * l + c + 1)
                    take((p, "b", c))
                    done(dve.tensor_tensor(F1[:, c, 0:n], pf((p, "b", c)), tmp[:, 0:n], ALU.mult))
                    emptied((p, "b", c))
                dve.wait_ge(sgb_in, 16 * (p + 1))
                for c in range(KC):
                    take((p, "mx", c))
                    out = pf((p, "mx", c))
                    ch.mark(dve.tensor_tensor(tmp[:, 0:GC].rearrange("p (t n) -> p t n", t=2),
                                              out[:, 0:GC].rearrange("p (t n) -> p t n", t=2),
                                              sg_b[:, c, :].unsqueeze(1).to_broadcast([P, 2, P]), ALU.add))
                    if g:
                        ch.mark(dve.tensor_tensor(ts, out[:, GC:NM].rearrange("p (b n) -> p b n", b=NSEQ),
                                                  sg_b[:, c, 0:NDEC].unsqueeze(1).to_broadcast([P, NSEQ, NDEC]), ALU.add))
                    ch.wait()
                    emptied((p, "u", c))
                    done(dve.tensor_tensor(F2[:, c, 0:n], F2[:, c, 0:n], tmp[:, 0:n], ALU.mult))
                    emptied((p, "mx", c))
                if g:
                    dve.wait_ge(vn_out, 16 * (l + 1))
                for c in range(KC):
                    emptied((p, "ga", c))
                    take((p, "oa", c))
                    done(dve.tensor_tensor(mT[:, c, 0:n], pf((p, "oa", c)), cs[0][:, 0:n], ALU.mult))
                    emptied((p, "gb", c))
                    take((p, "ob", c))
                    ch.link(dve.tensor_tensor(tmp[:, 0:n], pf((p, "ob", c)), cs[1][:, 0:n], ALU.mult))
                    emptied((p, "oa", c))
                    done(dve.tensor_tensor(mT[:, c, 0:n], mT[:, c, 0:n], tmp[:, 0:n], ALU.add))
                    emptied((p, "ob", c))

                def add_to_x(kind):
                    for i, (t, rows) in enumerate(tiles):
                        take((p, kind, i))
                        done(dve.tensor_tensor(X[0:rows, t, :], X[0:rows, t, :], pt((p, kind, i), rows), ALU.add))

                add_to_x("mo")
                if not g:
                    dve.wait_ge(mem_std, l + 1)
                    ch.link(dve.reciprocal(rstd[:, 5:7], std[:, 5:7]))
                    for m in range(MC):
                        ins = dve.tensor_scalar(mem[:, m, :], mem[:, m, :], rstd[:, 5 + m:6 + m], None, ALU.mult)
                    ins.then_inc(mem_norm, 1)
                    for m in range(MC):
                        take((p, "mt", m))
                        done(dve.tensor_tensor(memT[:, :, m * P:(m + 1) * P], chunks(pt((p, "mt", m))),
                                               gain(2).unsqueeze(2).to_broadcast([P, KC, P]), ALU.mult))
                for m in range(MC):
                    take((p, "kt", m))
                    done(dve.tensor_copy(kT[:, :, m * P:(m + 1) * P], chunks(pt((p, "kt", m)))))
                norm(1)

                def maxima(i, rows, name):
                    peer_to(AHEAD[name])
                    await_job(dve, name)
                    ch.link(dve.tensor_reduce(rmax[0:rows, i, :], pt(name, rows).rearrange("p (h m) -> p h m", h=HEADS), AX, ALU.max))
                    dve.tensor_scalar(nmax[0:rows, i, :], rmax[0:rows, i, :], -1.0 / 16.0, None, ALU.mult).then_inc(max_done, 1)

                def normalise(i, rows, name):
                    emptied(name)
                    ch.link(dve.reciprocal(rinv[0:rows, i, :], rsum[0:rows, i, :]))
                    pr = probs[i % 2][0:rows, :].rearrange("p (h m) -> p h m", h=HEADS)
                    dve.tensor_tensor(pr, pr, rinv[0:rows, i, :].unsqueeze(2).to_broadcast([rows, HEADS, NMEM]), ALU.mult).then_inc(prob_done, 1)

                maxima(0, P, (p, "s", 0))
                maxima(1, P, (p, "s", 1))
                normalise(0, P, (p, "s", 0))
                normalise(1, P, (p, "s", 1))
                if g:
                    for b in range(NSEQ):
                        take((p, "kb", b, 1))
                        done(dve.tensor_copy(kbT[b % 2][:, :, P:2 * P], chunks(pt((p, "kb", b, 1)))))
                    maxima(2, NS, (p, "sb"))
                    normalise(2, NS, (p, "sb"))
                    for b in range(NSEQ):
                        take((p, "os", b))
                        done(dve.tensor_copy(oT[:, :, GC + b * NDEC:GC + (b + 1) * NDEC], chunks(ps[:, BANK[p, "os", b], 0:KC * NDEC])))
                add_to_x("xo")
                for i in range(2):
                    take((p, "sk", i))
                    if not g:
                        dve.wait_ge(v_out, 32 * (l + 1))
                    done(dve.tensor_copy(skT[:, 8 * i:8 * i + 8, :], chunks(pt((p, "sk", i)))))
                norm(2)

            def all_top_k(p):
                emptied(LAST_SC[p])
                for i in range(len(GROUPS[p % 2])):
                    top_k(p, i)

            ch.mark(dve.memset(eps[:, :], EPS))
            ch.mark(dve.memset(ssq[:, :], 1.0))
            ch.mark(dve.memset(std[:, :], 1.0))
            ch.mark(dve.memset(bna[:, :, :], 1.0))
            ch.wait()
            dve.wait_ge(const_done, 1)
            dve.sem_inc(const_done, 1)
            dve.wait_ge(x_in, 32)
            for p in range(2 * DEPTH):
                if p:
                    all_top_k(p - 1)
                trunk(p)
            assert len(seen) == len(mine)
            all_top_k(2 * DEPTH - 1)
            peer_to(len(peer_groups))
            dve.wait_ge(sq_done, 3 * 2 * DEPTH + 1)
            ch.link(dve.reciprocal(rstd[:, 0:NTILE], std[:, 0:NTILE]))
            dve.wait_ge(ffn_in, 16 * (2 * DEPTH + 1))
            for t in range(NTILE):
                rows = NS if t == 4 else P
                dve.scalar_tensor_tensor(out=final_place(t), in0=X[0:rows, t, :], scalar=rstd[0:rows, t:t + 1],
                                         in1=ffn_g[0:rows, :], op0=ALU.mult, op1=ALU.mult).then_inc(y_done, 1)


_INS = ["x_prompt", "x_sample", "state_conv", "cache_mem_k", "cache_mem_v", "mem_prompt", "g_mix", "w_in", "conv_w",
        "w_a_out", "sg_ln_g", "sg_ln_b", "sg_w", "sg_b", "w_b_out", "w_mix_o", "g_xattn", "g_mem", "w_xq", "w_xk",
        "w_xv", "w_xo", "g_ffn", "w_pq", "sub_keys", "peer_u", "peer_v", "g_final"]
_OUTS = [("y_prompt", (1, SEQ, DM)), ("y_sample", (NSEQ, NDEC, DM)),
         ("new_state_conv_p", (DEPTH, 1, CW - 1, DM)), ("new_mem_k_p", (DEPTH, 1, NMEM, HEADS, HD)),
         ("new_mem_v_p", (DEPTH, 1, NMEM, HEADS, HD)), ("new_state_conv_s", (DEPTH, NSEQ, CW - 1, DM)),
         ("new_sg_v_s", (DEPTH, NSEQ, NDEC, DM))]


def kernel(**inputs):
    import numpy as _np
    import concourse.bacc as _bacc
    from concourse import mybir as _mybir
    from concourse.bass_utils import run_bass_kernel_spmd as _run

    nc = _bacc.Bacc("TRN2", target_bir_lowering=False, num_devices=1)
    arrays, ins, outs = {}, {}, {}
    for name in _INS:
        a = _np.ascontiguousarray(inputs[name])
        arrays[f"in_{name}_dram"] = a
        ins[name] = nc.dram_tensor(f"in_{name}_dram", a.shape, _mybir.dt.from_np(a.dtype), kind="ExternalInput").ap()
    for name, shape in _OUTS:
        outs[name] = nc.dram_tensor(f"out_{name}_dram", shape, F32, kind="ExternalOutput").ap()
    decoder_step(nc, ins, outs)
    r = _run(nc, [arrays], core_ids=[0])
    return tuple(r.results[0][f"out_{name}_dram"] for name, _ in _OUTS)
```
